# Optimizing a Trainium2 kernel written in Bass

```python
import math
import jax
import jax.numpy as jnp
from jax import lax
import numpy as np

D_MODEL = 1024
BATCH = 1
SEQ = 256
DEPTH = 1
DEC_BATCH = 8
DEC_SEQ = 8
PAST_LEN = 2048
PAGE_SIZE = 128

H_A = 4
DK_A = 128
DV_A = 128
W_A = H_A * DV_A
CONV_W = 4
CONV_DIM = 2 * H_A * DK_A + W_A
GDN_CHUNK = 64
H_B = 4
DK_B = 64
DV_B = 128
W_B = H_B * DV_B
GK_RANK = 16
GLA_GATE_NORM = 16.0
GLA_CHUNK = 16
N_EXPERTS = 32
TOP_K = 4
D_FF = 1024
SWIGLU_LIMIT = 7.0
SWIGLU_ALPHA = 1.702
MOE_BLOCK = 128
RMS_EPS = 1e-6
IN_SIZES = (CONV_DIM, W_A, H_A, H_A, H_B * DK_B, H_B * DK_B, W_B, W_B, GK_RANK, D_MODEL, D_MODEL)
IN_DIM = sum(IN_SIZES)

kernel_name = "hybrid_gdn_gla_moe_step"

def _rms(x, w):
    xf = x.astype(jnp.float32)
    y = xf * lax.rsqrt(jnp.mean(xf * xf, axis=-1, keepdims=True) + RMS_EPS) * w.astype(jnp.float32)
    return y.astype(x.dtype)

def _l2norm(x):
    return x * lax.rsqrt(jnp.sum(x * x, axis=-1, keepdims=True) + 1e-6)

def _gated_head_rms(o, z, w):
    r = o * lax.rsqrt(jnp.mean(o * o, axis=-1, keepdims=True) + RMS_EPS) * w.astype(jnp.float32)
    return r * jax.nn.silu(z.astype(jnp.float32))

def _chunk_len(t, c):
    return math.gcd(t, c)

def _to_chunks(a, c):
    b, t = a.shape[:2]
    return jnp.swapaxes(a.reshape((b, t // c, c) + a.shape[2:]), 2, 3)

def _from_chunks(o):
    n, b, h, c, d = o.shape
    return jnp.transpose(o, (1, 0, 3, 2, 4)).reshape(b, n * c, h, d)

def _short_conv(u, buf, w):
    t = u.shape[1]
    ucat = jnp.concatenate([buf.astype(u.dtype), u], axis=1)
    y = ucat[:, 0:t] * w[0]
    for j in range(1, CONV_W):
        y = y + ucat[:, j:j + t] * w[j]
    return jax.nn.silu(y), ucat[:, -(CONV_W - 1):]

def _gated_delta_rule(q, k, v, g, beta, s0):
    t = q.shape[1]
    c = _chunk_len(t, GDN_CHUNK)
    qc, kc, vc = _to_chunks(q, c), _to_chunks(k, c), _to_chunks(v, c)
    gc = jnp.cumsum(_to_chunks(g, c), axis=-1)
    bc = _to_chunks(beta, c)
    tri = jnp.tril(jnp.ones((c, c), bool))
    strict = jnp.tril(jnp.ones((c, c), bool), -1)
    diff = gc[..., :, None] - gc[..., None, :]
    decay = jnp.where(tri, jnp.exp(jnp.where(tri, diff, 0.0)), 0.0)
    kb = kc * bc[..., None]
    vb = vc * bc[..., None]
    lower = jnp.where(strict, jnp.einsum('bnhid,bnhjd->bnhij', kb, kc) * decay, 0.0)
    amat = lower + jnp.eye(c, dtype=lower.dtype)
    rhs = jnp.concatenate([vb, kb * jnp.exp(gc)[..., None]], axis=-1)
    sol = lax.linalg.triangular_solve(amat, rhs, left_side=True, lower=True, unit_diagonal=True)
    u, w = sol[..., :DV_A], sol[..., DV_A:]
    attn = jnp.where(tri, jnp.einsum('bnhid,bnhjd->bnhij', qc, kc) * decay, 0.0)
    qg = qc * jnp.exp(gc)[..., None]
    kd = kc * jnp.exp(gc[..., -1:] - gc)[..., None]
    glast = jnp.exp(gc[..., -1])

    def step(s, xs):
        u_i, w_i, attn_i, qg_i, kd_i, gl_i = xs
        v_new = u_i - jnp.einsum('bhcd,bhde->bhce', w_i, s)
        o = jnp.einsum('bhcd,bhde->bhce', qg_i, s) + jnp.einsum('bhij,bhje->bhie', attn_i, v_new)
        s = s * gl_i[..., None, None] + jnp.einsum('bhcd,bhce->bhde', kd_i, v_new)
        return s, o

    xs = tuple(jnp.moveaxis(a, 1, 0) for a in (u, w, attn, qg, kd, glast))
    s_fin, o = lax.scan(step, s0, xs)
    return _from_chunks(o), s_fin

def _gla(q, k, v, log_a, s0):
    t = q.shape[1]
    c = _chunk_len(t, GLA_CHUNK)
    qc, kc, vc = _to_chunks(q, c), _to_chunks(k, c), _to_chunks(v, c)
    gcum = jnp.cumsum(_to_chunks(log_a, c), axis=3)
    tri = jnp.tril(jnp.ones((c, c), bool))
    qg = qc * jnp.exp(gcum)
    kg = kc * jnp.exp(-gcum)
    attn = jnp.where(tri, jnp.einsum('bnhid,bnhjd->bnhij', qg, kg), 0.0)
    o_intra = jnp.einsum('bnhij,bnhje->bnhie', attn, vc)
    kd = kc * jnp.exp(gcum[..., -1:, :] - gcum)
    glast = jnp.exp(gcum[..., -1, :])

    def step(s, xs):
        qg_i, kd_i, v_i, gl_i = xs
        o = jnp.einsum('bhcd,bhde->bhce', qg_i, s)
        s = s * gl_i[..., None] + jnp.einsum('bhcd,bhce->bhde', kd_i, v_i)
        return s, o

    xs = tuple(jnp.moveaxis(a, 1, 0) for a in (qg, kd, vc, glast))
    s_fin, o_inter = lax.scan(step, s0, xs)
    return _from_chunks(o_inter) + _from_chunks(jnp.moveaxis(o_intra, 1, 0)), s_fin

def _moe(x2d, w_router, b_router, w_gate_up, b_gate_up, w_down, b_down):
    n, d = x2d.shape
    logits = (x2d @ w_router).astype(jnp.float32) + b_router.astype(jnp.float32)
    top_v, top_e = lax.top_k(logits, TOP_K)
    gates = jax.nn.softmax(top_v, axis=-1)
    n_assign = n * TOP_K
    flat_e = top_e.reshape(-1)
    order = jnp.argsort(flat_e)
    e_sorted = flat_e[order]
    tok_sorted = (order // TOP_K).astype(jnp.int32)
    counts = jnp.zeros((N_EXPERTS,), jnp.int32).at[flat_e].add(1)
    padded = (counts + MOE_BLOCK - 1) // MOE_BLOCK * MOE_BLOCK
    pad_end = jnp.cumsum(padded)
    pad_start = pad_end - padded
    start = jnp.cumsum(counts) - counts
    dest = pad_start[e_sorted] + jnp.arange(n_assign, dtype=jnp.int32) - start[e_sorted]
    n_blocks = -(-n_assign // MOE_BLOCK) + N_EXPERTS
    rows = n_blocks * MOE_BLOCK
    row_tok = jnp.full((rows,), n, jnp.int32).at[dest].set(tok_sorted)
    blk_expert = jnp.minimum(
        jnp.searchsorted(pad_end, jnp.arange(n_blocks, dtype=jnp.int32) * MOE_BLOCK, side='right'),
        N_EXPERTS - 1)
    xpad = jnp.concatenate([x2d, jnp.zeros((1, d), x2d.dtype)], axis=0)
    xb = xpad[row_tok].reshape(n_blocks, MOE_BLOCK, d)

    def expert_block(args):
        xblk, e = args
        gu = xblk @ w_gate_up[e] + b_gate_up[e]
        gate, up = gu[..., :D_FF], gu[..., D_FF:]
        gate = jnp.minimum(gate, SWIGLU_LIMIT)
        up = jnp.clip(up, -SWIGLU_LIMIT, SWIGLU_LIMIT)
        hmid = (up + 1.0) * (gate * jax.nn.sigmoid(SWIGLU_ALPHA * gate))
        return hmid @ w_down[e] + b_down[e]

    yb = lax.map(expert_block, (xb, blk_expert)).reshape(rows, d)
    w_sorted = gates.reshape(-1)[order].astype(yb.dtype)
    return jnp.zeros((n, d), yb.dtype).at[tok_sorted].add(yb[dest] * w_sorted[:, None])

def _layer(x, s_gdn, s_conv, s_gla, norm1_w, w_in, conv_w, a_log, dt_bias, gdn_norm_w,
           gla_gk_up, gla_gk_b, gla_norm_w, w_up_a, w_up_b, w_o, norm2_w,
           w_router, b_router, w_gate_up, b_gate_up, w_down, b_down):
    b, t, _ = x.shape
    f32 = jnp.float32
    h = _rms(x, norm1_w)
    p = h @ w_in
    split_idx = np.cumsum(IN_SIZES)[:-1].tolist()
    (qkv_a, z_a, alpha_a, beta_a, q_b, k_b, v_b, g_b, gk_lr, gate_a, gate_b) = jnp.split(p, split_idx, axis=-1)

    qkv_a, new_conv = _short_conv(qkv_a, s_conv, conv_w)
    qkv_a = qkv_a.astype(f32)
    qa = _l2norm(qkv_a[..., :H_A * DK_A].reshape(b, t, H_A, DK_A)) * (DK_A ** -0.5)
    ka = _l2norm(qkv_a[..., H_A * DK_A:2 * H_A * DK_A].reshape(b, t, H_A, DK_A))
    va = qkv_a[..., 2 * H_A * DK_A:].reshape(b, t, H_A, DV_A)
    g = -jnp.exp(a_log.astype(f32)) * jax.nn.softplus(alpha_a.astype(f32) + dt_bias.astype(f32))
    beta = jax.nn.sigmoid(beta_a.astype(f32))
    o_a, new_gdn = _gated_delta_rule(qa, ka, va, g, beta, s_gdn.astype(f32))
    o_a = _gated_head_rms(o_a, z_a.reshape(b, t, H_A, DV_A), gdn_norm_w).reshape(b, t, W_A).astype(x.dtype)

    gk = (gk_lr @ gla_gk_up + gla_gk_b).astype(f32).reshape(b, t, H_B, DK_B)
    log_a = jax.nn.log_sigmoid(gk) / GLA_GATE_NORM
    qb = q_b.astype(f32).reshape(b, t, H_B, DK_B) * (DK_B ** -0.5)
    kb = k_b.astype(f32).reshape(b, t, H_B, DK_B)
    vb = v_b.astype(f32).reshape(b, t, H_B, DV_B)
    o_b, new_gla = _gla(qb, kb, vb, log_a, s_gla.astype(f32))
    o_b = _gated_head_rms(o_b, g_b.reshape(b, t, H_B, DV_B), gla_norm_w).reshape(b, t, W_B).astype(x.dtype)

    merged = jax.nn.sigmoid(gate_a) * (o_a @ w_up_a) + jax.nn.sigmoid(gate_b) * (o_b @ w_up_b)
    x = x + merged @ w_o

    h2 = _rms(x, norm2_w).reshape(b * t, D_MODEL)
    x = x + _moe(h2, w_router, b_router, w_gate_up, b_gate_up, w_down, b_down).reshape(b, t, D_MODEL)
    return x, new_gdn.astype(s_gdn.dtype), new_conv.astype(s_conv.dtype), new_gla.astype(s_gla.dtype)

def _trunk(x, s_gdn, s_conv, s_gla, norm1_w, w_in, conv_w, a_log, dt_bias, gdn_norm_w,
           gla_gk_up, gla_gk_b, gla_norm_w, w_up_a, w_up_b, w_o, norm2_w,
           w_router, b_router, w_gate_up, b_gate_up, w_down, b_down, norm_f_w):
    gdn_out, conv_out, gla_out = [], [], []
    for l in range(DEPTH):
        x, sg, sc, sl = _layer(x, s_gdn[l], s_conv[l], s_gla[l], norm1_w[l], w_in[l], conv_w[l],
                               a_log[l], dt_bias[l], gdn_norm_w[l], gla_gk_up[l], gla_gk_b[l],
                               gla_norm_w[l], w_up_a[l], w_up_b[l], w_o[l], norm2_w[l],
                               w_router[l], b_router[l], w_gate_up[l], b_gate_up[l],
                               w_down[l], b_down[l])
        gdn_out.append(sg)
        conv_out.append(sc)
        gla_out.append(sl)
    return _rms(x, norm_f_w), jnp.stack(gdn_out), jnp.stack(conv_out), jnp.stack(gla_out)

def setup_inputs(seed: int = 0) -> dict:
    key = jax.random.key(seed)
    ks = jax.random.split(key, 32)
    f32 = jnp.float32

    def nrm(k, shape, scale):
        return jax.random.normal(k, shape, f32) * scale

    L = DEPTH
    dt = jnp.exp(jax.random.uniform(ks[9], (L, H_A), f32, math.log(1e-3), math.log(1e-1)))
    return {
        "x_prompt": nrm(ks[0], (BATCH, SEQ, D_MODEL), 1.0),
        "x_sample": nrm(ks[1], (DEC_BATCH, DEC_SEQ, D_MODEL), 1.0),
        "state_gdn": nrm(ks[2], (L, DEC_BATCH, H_A, DK_A, DV_A), 0.5),
        "state_gdn_conv": nrm(ks[3], (L, DEC_BATCH, CONV_W - 1, CONV_DIM), 1.0),
        "state_gla": nrm(ks[4], (L, DEC_BATCH, H_B, DK_B, DV_B), 0.5),
        "norm1_w": 1.0 + nrm(ks[5], (L, D_MODEL), 0.02),
        "w_in": nrm(ks[6], (L, D_MODEL, IN_DIM), D_MODEL ** -0.5),
        "conv_w": nrm(ks[7], (L, CONV_W, CONV_DIM), CONV_W ** -0.5),
        "a_log": jnp.log(jax.random.uniform(ks[8], (L, H_A), f32, 1.0, 16.0)),
        "dt_bias": dt + jnp.log(-jnp.expm1(-dt)),
        "gdn_norm_w": 1.0 + nrm(ks[10], (L, DV_A), 0.02),
        "gla_gk_up": nrm(ks[11], (L, GK_RANK, H_B * DK_B), GK_RANK ** -0.5),
        "gla_gk_b": nrm(ks[12], (L, H_B * DK_B), 0.01),
        "gla_norm_w": 1.0 + nrm(ks[13], (L, DV_B), 0.02),
        "w_up_a": nrm(ks[14], (L, W_A, D_MODEL), W_A ** -0.5),
        "w_up_b": nrm(ks[15], (L, W_B, D_MODEL), W_B ** -0.5),
        "w_o": nrm(ks[16], (L, D_MODEL, D_MODEL), D_MODEL ** -0.5),
        "norm2_w": 1.0 + nrm(ks[17], (L, D_MODEL), 0.02),
        "w_router": nrm(ks[18], (L, D_MODEL, N_EXPERTS), D_MODEL ** -0.5),
        "b_router": nrm(ks[19], (L, N_EXPERTS), 0.01),
        "w_gate_up": nrm(ks[20], (L, N_EXPERTS, D_MODEL, 2 * D_FF), D_MODEL ** -0.5),
        "b_gate_up": nrm(ks[21], (L, N_EXPERTS, 2 * D_FF), 0.01),
        "w_down": nrm(ks[22], (L, N_EXPERTS, D_FF, D_MODEL), D_FF ** -0.5),
        "b_down": nrm(ks[23], (L, N_EXPERTS, D_MODEL), 0.01),
        "norm_f_w": 1.0 + nrm(ks[24], (D_MODEL,), 0.02),
    }

def reference(x_prompt, x_sample, state_gdn, state_gdn_conv, state_gla, norm1_w, w_in, conv_w,
              a_log, dt_bias, gdn_norm_w, gla_gk_up, gla_gk_b, gla_norm_w, w_up_a, w_up_b, w_o,
              norm2_w, w_router, b_router, w_gate_up, b_gate_up, w_down, b_down, norm_f_w):
    dt = x_prompt.dtype
    zg = jnp.zeros((DEPTH, BATCH, H_A, DK_A, DV_A), dt)
    zc = jnp.zeros((DEPTH, BATCH, CONV_W - 1, CONV_DIM), dt)
    zl = jnp.zeros((DEPTH, BATCH, H_B, DK_B, DV_B), dt)
    y_prompt, gdn_p, conv_p, gla_p = _trunk(
        x_prompt, zg, zc, zl, norm1_w, w_in, conv_w, a_log, dt_bias, gdn_norm_w, gla_gk_up,
        gla_gk_b, gla_norm_w, w_up_a, w_up_b, w_o, norm2_w, w_router, b_router, w_gate_up,
        b_gate_up, w_down, b_down, norm_f_w)
    y_sample, gdn_s, conv_s, gla_s = _trunk(
        x_sample, state_gdn, state_gdn_conv, state_gla, norm1_w, w_in, conv_w, a_log, dt_bias,
        gdn_norm_w, gla_gk_up, gla_gk_b, gla_norm_w, w_up_a, w_up_b, w_o, norm2_w, w_router,
        b_router, w_gate_up, b_gate_up, w_down, b_down, norm_f_w)
    return (y_prompt, y_sample, gdn_p, conv_p, gla_p, gdn_s, conv_s, gla_s)


_drawn_inputs = setup_inputs


def setup_inputs(seed=0):
    import zlib

    import numpy as np

    out = dict(_drawn_inputs(seed))
    spreads = {}
    factors = {'gla_gk_b': 8.0, 'b_gate_up': 8.0, 'b_down': 8.0, 'norm_f_w': 2.849}
    for name, (base, spread) in spreads.items():
        noise = np.random.default_rng([zlib.crc32(name.encode()), seed]).standard_normal(out[name].shape)
        drawn = base * np.exp(spread * noise) if base else spread * noise
        out[name] = jnp.asarray(drawn.astype(out[name].dtype))
    for name, factor in factors.items():
        out[name] = (out[name] * factor).astype(out[name].dtype)
    return out
```

```python
from contextlib import ExitStack

import concourse.bass as bass
from concourse import mybir

F32 = mybir.dt.float32
U32 = mybir.dt.uint32
I32 = mybir.dt.int32
ALU = mybir.AluOpType
ACT = mybir.ActivationFunctionType
AX_X = mybir.AxisListType.X

D = 1024
KD = D // 128
HEADS = 4
DK_A, DV = 128, 128
DK_B = 64
QKV = 3 * HEADS * 128
QT = QKV // 128
PROMPT, BATCHES, STEPS = 256, 8, 8
TOK = PROMPT + BATCHES * STEPS
TILE_N = [128, 128, 64]
TILE_0 = [0, 128, 256]
RANK = 16
EXPERTS, TOP, FF = 32, 4, 1024
FT = FF // 128
EPS = 1e-6
GATE_NORM = 16.0
LIMIT, ALPHA = 7.0, 1.702
SLOTS = 64
ROUNDS = TOK // SLOTS
PAIRS = EXPERTS // 2
CATN = 3 + PROMPT + BATCHES * (3 + STEPS)
CATS = 3 + PROMPT
CONVN = CATN - 3

C_QKV, C_Z, C_AB = 0, 1536, 2048
C_QB, C_KB, C_VB, C_GB, C_LR, C_GA, C_GBB = 2056, 2312, 2568, 3080, 3592, 3608, 4632

RING = 12
MIX = 6
MIX_PANELS = 30
MIX_USES = MIX_PANELS // MIX

LEVELS = [1, 2, 4, 8, 16, 32, 64]


def levels_of(s):
    return LEVELS if s < 2 else LEVELS[:3]


def psum_order():
    o = ["cols", "cst"]
    o += [f"xT{s}{f}" for s in range(3) for f in range(2)]
    o += [f"qkv{t}" for t in range(QT)]
    o += ["ab", "lr"]
    o += [f"z{t}" for t in range(4)] + [f"qb{t}" for t in range(2)] + [f"kb{t}" for t in range(2)]
    o += ["gk0", "gk1"] + [f"tail{g}" for g in range(3)]
    o += [f"vb{s}" for s in range(3)] + [f"g{t}" for t in range(4)]
    o += [f"nrm{t}" for t in range(8)]
    o += ["gc"]
    for h in range(HEADS):
        o += [f"gB{h}", f"bB{h}"]
    o += [f"kT{s}" for s in range(3)]
    for s in range(3):
        o += [f"A{s}", f"Q{s}"]
    o += [f"t2{s}" for s in range(3)]
    for b in LEVELS[1:]:
        for s in range(3):
            if b in levels_of(s):
                o += [f"X{s}{b}"]
        for s in range(3):
            if b in levels_of(s):
                o += ([f"Y{s}{b}"] if b != levels_of(s)[-1] else []) + [f"Z{s}{b}"]
    o += ["rt0", "v0", "o0", "s0", "ks1", "rt1", "v1", "o1", "s1", "ks2", "rt2", "v2", "o2"]
    o += [f"ss{h}{f}" for h in range(HEADS) for f in range(2)]
    o += [f"on{h}" for h in range(HEADS)]
    for lv in range(4):
        o += [f"L{lv}{s}{r}" for s in range(3 if lv == 0 else 2) for r in range(2)]
    o += [f"gT{s}" for s in range(3)]
    o += ["ob00", "ob01", "gs0", "ob10", "ob11", "gs1", "ob20", "ob21"]
    o += [f"gss{h}{f}" for h in range(HEADS) for f in range(2)]
    o += [f"om{h}" for h in range(HEADS)]
    for m in range(KD):
        o += [f"ga{m}", f"gb{m}", f"ua{m}", f"ub{m}"]
    o += [f"wo{s}{f}" for s in range(3) for f in range(2)]
    o += [f"hT{s}{f}" for s in range(3) for f in range(2)]
    o += [f"lg{s}" for s in range(3)]
    o += [f"sl{s}" for s in range(3)] + ["cnt", "wT", "bgu"]
    o += [f"bd{s}{f}" for s in range(3) for f in range(2)]
    return o


PSUM_USE = {name: (i % 8, i // 8) for i, name in enumerate(psum_order())}


def build(nc, x_prompt, x_sample, state_gdn, state_gdn_conv, state_gla, norm1_w, w_in, conv_w, a_log, dt_bias,
          gdn_norm_w, gla_gk_up, gla_gk_b, gla_norm_w, w_up_a, w_up_b, w_o, norm2_w, w_router, b_router,
          w_gate_up, b_gate_up, w_down, b_down, norm_f_w, y_prompt, y_sample, gdn_p, conv_p, gla_p, gdn_s,
          conv_s, gla_s):
    with ExitStack() as ctx:
        def sb(name, shape, dt=F32):
            return ctx.enter_context(nc.sbuf_tensor(name, shape, dt))

        def sem(name):
            return ctx.enter_context(nc.semaphore(name))

        def flat(t, a, shape):
            n = 1
            for k in shape:
                n *= k
            v = t[:, a:a + n]
            if len(shape) == 1:
                return v
            names = "abcd"[:len(shape)]
            return v.rearrange("p (" + " ".join(names) + ") -> p " + " ".join(names),
                               **dict(zip(names[1:], shape[1:])))

        ring = sb("ring", [128, RING * 2048])

        def slot(i):
            return ring[:, i * 2048:(i + 1) * 2048]

        W0 = MIX * 2048
        AT = flat(ring, W0, (3, HEADS, 128))
        attnT = flat(ring, W0 + 1536, (3, HEADS, 128))
        kbqg = flat(ring, W0 + 3072, (2, HEADS, TOK))
        W1 = W0 + 3072 + 2560
        cat = flat(ring, W1, (QT, CATN))
        T_ = flat(ring, W1, (3, HEADS, 128))
        TT = flat(ring, W1 + 1536, (3, HEADS, 128))
        X1 = flat(ring, W1 + 3072, (3, HEADS, 128))
        LT = flat(ring, W1 + 4608, (3, HEADS, 128))
        assert W1 + 6144 + 512 <= RING * 2048
        eq = flat(ring, W1, (2, TOK))
        ek = flat(ring, W1 + 640, (2, TOK))
        qt = flat(ring, W1 + 1280, (2, 2, TOK))
        kt = flat(ring, W1 + 2560, (2, 2, TOK))
        qG = flat(ring, W1 + 3840, (2, TOK))
        kdF = flat(ring, W1 + 4480, (2, TOK))
        VM = flat(ring, W0 + 3072, (BATCHES, 128))
        kdG = flat(ring, W0 + 1536, (3, 2, 128))
        osq = flat(ring, W1 + 1280, (HEADS, TOK))
        Lp = flat(ring, W1 + 5120, (HEADS, 128))

        xbuf = sb("xbuf", [128, 3 * D])
        x_tm = flat(xbuf, 0, (3, D))
        R = flat(xbuf, 0, (3, HEADS, 128))
        kdT = flat(xbuf, 1536, (3, HEADS, 128))
        tail_tm = flat(xbuf, 1536, (QKV,))
        hTb = sb("hTb", [128, KD * TOK])
        hT = flat(hTb, 0, (KD, TOK))
        h2b = sb("h2b", [128, QT * TOK])
        qkv = flat(h2b, 0, (QT, TOK))
        merged = flat(h2b, 0, (KD, TOK))
        zgb = sb("zgb", [128, 8 * TOK])
        zg = flat(zgb, 0, (8, TOK))
        cst_rows = zgb[0:24, 0:QKV]
        qb = sb("qb", [128, 2 * TOK])
        kb = sb("kb", [128, 2 * TOK])
        Gc = sb("Gc", [128, 2 * TOK])
        qb3, kb3, G3 = (flat(t, 0, (2, TOK)) for t in (qb, kb, Gc))
        vTM = sb("vTM", [128, 3, 512])
        oAb = sb("oAb", [128, HEADS * TOK])
        oBb = sb("oBb", [128, HEADS * TOK])
        oA = flat(oAb, 0, (HEADS, TOK))
        oB = flat(oBb, 0, (HEADS, TOK))
        Sg = sb("Sg", [128, BATCHES * HEADS, 128])
        bcol = Sg[:, 12:16, :].rearrange("p a b -> p (a b)")
        Sl = sb("Sl", [128, BATCHES * 2, 128])
        Sp = sb("Sp", [128, HEADS, 128])
        Slp = sb("Slp", [128, 2, 128])
        cv = sb("cv", [128, 2, CATN])
        tails = flat(ring, W0 + 768, (QT, 27))
        rows = sb("rows", [64, 128])
        cols = sb("cols", [128, 64])
        w_small = flat(ring, W0, (KD, 24))
        gk_up = ring[0:RANK, W0 + 192:W0 + 448]
        lrT = ring[0:RANK, W0 + 448:W0 + 768]
        ab = sb("ab", [128, 3, 8])
        hb = sb("hb", [128, 8])
        u_dt = sb("u_dt", [128, 3, HEADS])
        absu = sb("absu", [128, 3, HEADS])
        soft = sb("soft", [128, 3, HEADS])
        beta = sb("beta", [128, 3, HEADS])
        g_tm = sb("g_tm", [128, 3, HEADS])
        kdf = sb("kdf", [128, 3, HEADS])
        glp = sb("glp", [128, 2, HEADS])
        glb = sb("glb", [128, HEADS, BATCHES])
        gll = sb("gll", [128, 2, 10])
        gneg = sb("gneg", [128, 3, HEADS])
        ss = sb("ss", [128, 8])
        rs = sb("rs", [128, 8])
        rt8 = sb("rt8", [128, 3, 8])
        ri8 = sb("ri8", [128, 3, 8], U32)
        rif = sb("rif", [128, 3, 8])
        rg4 = sb("rg4", [128, 3, 4])
        rneg = sb("rneg", [128, 3, 2])
        lgt = sb("lgt", [128, 3, EXPERTS])
        msk = sb("msk", [128, 3, EXPERTS])
        tmp32 = sb("tmp32", [128, EXPERTS])
        cmax = sb("cmax", [128, 8])
        nit = sb("nit", [128, 2], I32)
        wr = sb("wr", [128, KD, EXPERTS])
        brt = sb("brt", [128, EXPERTS])

        ident = sb("ident", [128, 128])
        ones = sb("ones", [128, 128])
        triu = sb("triu", [128, 128])
        blk = flat(ring, W0 + 1536, (6, 128))
        lvm_hi = sb("lvm_hi", [128, 3, 128])
        lvm_lo = flat(ring, W1 + 6144, (4, 128))
        lvm = [lvm_lo[:, i, :] for i in range(4)] + [lvm_hi[:, i, :] for i in range(3)]
        tri8 = sb("tri8", [128, 128])
        tri16 = sb("tri16", [128, 128])
        b8 = sb("b8", [64, 64])
        bsel = sb("bsel", [128, BATCHES])
        rst = sb("rst", [128, TOK])
        eps = sb("eps", [128, 1])
        iota = sb("iota", [128, SLOTS])

        bank = [ctx.enter_context(nc.psum_tensor(f"bank{i}", [128, 512], F32)) for i in range(8)]

        wfull = [sem(f"wfull{i}") for i in range(RING)]
        wfree = [sem(f"wfree{i}") for i in range(RING)]
        pfull = [sem(f"pfull{i}") for i in range(8)]
        pfree = [sem(f"pfree{i}") for i in range(8)]
        s_x, s_rows, s_small, s_misc, s_state = (sem(n) for n in (
            "x_in", "rows_in", "small_in", "misc_in", "state_in"))
        s_x2, s_late = sem("x_again"), sem("late_in")
        consts = sem("consts")
        act_c, dve_c, pool_c = sem("act_chain"), sem("dve_chain"), sem("pool_chain")
        rs_ready, xs_ready = sem("rs_ready"), sem("xs_ready")
        conv_done, silu_done = sem("conv_done"), sem("silu_done")
        tails_ready = sem("tails_ready")
        sq_ready, nrm_ready, qk_ready = sem("sq_ready"), sem("nrm_ready"), sem("qk_ready")
        ab_exp, ab_mid, g_ready = sem("ab_exp"), sem("ab_mid"), sem("g_ready")
        gneg_ready, dt_exp, kdf_ready, kb_ready = sem("gneg_ready"), sem("dt_exp"), sem("kdf_ready"), sem("kb_ready")
        dt_ready = sem("dt_ready")
        lt_ready, t2t_ready, inv_ready = sem("lt_ready"), sem("t2t_ready"), sem("inv_ready")
        rt_ready, vm_ready, st_ready = sem("rt_ready"), sem("vm_ready"), sem("st_ready")
        osq_ready, onr_ready, o_ready = sem("osq_ready"), sem("onr_ready"), sem("o_ready")
        la_act, la_ready, lev_sub, lev_exp, lev_ready = (sem(n) for n in (
            "la_act", "la_ready", "lev_sub", "lev_exp", "lev_ready"))
        at_ready, kd_ready = sem("at_ready"), sem("kd_ready")
        sig_ready, mrg_ready = sem("sig_ready"), sem("mrg_ready")
        x2_ready, x2_rs, h2_ready, route_max, route_exp, gate_ready, slot_ready, cnt_ready = (sem(n) for n in (
            "x2_ready", "x2_rs", "h2_ready", "route_max", "route_exp", "gate_ready", "slot_ready", "cnt_ready"))
        out_sem, y_out = sem("outputs"), sem("y_out")
        fin_act, fin_dve = sem("fin_act"), sem("fin_dve")
        m_full = [sem(f"mfull{i}") for i in range(8)]
        m_act, m_dve = sem("moe_act_chain"), sem("moe_dve_chain")
        xg_done, yt_done, t_full, gtr_done = sem("xg_done"), sem("yt_done"), sem("t_full"), sem("gtr_done")
        pre_done = sem("pre_done")
        acc_done, p_ready, gm_ready, hm_ready, sg_ready, pre_sig = (sem(n) for n in (
            "acc_done", "p_ready", "gm_ready", "hm_ready", "sg_ready", "pre_sig"))

        def bcast(col, shape):
            return col.to_broadcast(shape)

        def mid(ap2, n):
            return ap2.unsqueeze(1).to_broadcast([ap2.shape[0], n, ap2.shape[1]])

        def last(ap2, n):
            return ap2.unsqueeze(2).to_broadcast([ap2.shape[0], ap2.shape[1], n])

        def full(eng, name):
            b, u = PSUM_USE[name]
            eng.wait_ge(pfull[b], u + 1)
            return bank[b]

        def freed(eng, name):
            b, u = PSUM_USE[name]
            eng.wait_ge(pfree[b], u + 1)

        def chain(eng, own):
            count = {}

            def step(ins, signal=None):
                s = signal or own
                count[s.name] = count.get(s.name, 0) + 1
                ins.then_inc(s, 1)
                eng.wait_ge(s, count[s.name])

            def free(ins, name):
                b, u = PSUM_USE[name]
                ins.then_inc(pfree[b], 1)
                eng.wait_ge(pfree[b], u + 1)
            return step, free

        def p3(bk, a, b):
            return bk[:, 0:a * b].rearrange("p (a b) -> p a b", b=b)

        def win(c0, n=256):
            return w_in[0][:, c0:c0 + n].rearrange("(k p) n -> p k n", p=128)

        panels = [win(C_QKV + 256 * i) for i in range(6)] + [win(C_Z + 256 * i) for i in range(2)]
        panels += [win(C_QB), win(C_KB), win(C_VB), win(C_VB + 256), win(C_GB), win(C_GB + 256)]
        for f in range(2):
            panels += [w[0][:, 512 * f:512 * f + 512].rearrange("(k p) n -> p k n", p=128) for w in (w_up_a, w_up_b)]
            for i in range(2):
                panels += [win(C_GA + 256 * (2 * f + i)), win(C_GBB + 256 * (2 * f + i))]
        panels += [w_o[0][256 * i:256 * i + 256, :].rearrange("(k p) n -> p k n", p=128) for i in range(4)]
        assert len(panels) == MIX_PANELS
        last_use = [f"qkv{2 * i + 1}" for i in range(6)] + ["z1", "z3", "qb1", "kb1", "vb2", "vb2", "g1", "g3"]
        for f in range(2):
            last_use += [f"ua{4 * f + 3}", f"ub{4 * f + 3}"]
            last_use += [f"{nm}{4 * f + 2 * i + 1}" for i in range(2) for nm in ("ga", "gb")]
        last_use += ["wo21"] * 4
        P_Z, P_QB, P_KB, P_VB, P_GB, P_M, P_O = 6, 8, 9, 10, 12, 14, 26

        def expert_chunk(e, c):
            if c < 8:
                return w_gate_up[0][e, 128 * c:128 * c + 128, :] if isinstance(e, int) else \
                    w_gate_up[0][bass.ds(e, 1), 128 * c:128 * c + 128, :].rearrange("e p n -> p (e n)")
            r = 256 * (c - 8)
            if isinstance(e, int):
                return w_down[0][e, r:r + 256, :].rearrange("(k p) n -> p k n", p=128)
            return w_down[0][bass.ds(e, 1), r:r + 256, :].rearrange("e (k p) n -> p (e k) n", p=128)

        def chunk_dst(c):
            return slot(c) if c < 8 else slot(c).rearrange("p (k n) -> p k n", k=2)

        block = ctx.enter_context(nc.Block())

        @block.sync
        def _(sp):
            sp.dma_start(x_tm[:, 0:2, :], x_prompt[0].rearrange("(s p) d -> p s d", p=128)).then_inc(s_x, 16)
            sp.dma_start(x_tm[0:64, 2, :], x_sample.rearrange("b t d -> (b t) d")).then_inc(s_x, 16)
            sp.dma_start(rows[0:8, :], norm1_w[0].rearrange("(k p) -> k p", p=128)).then_inc(s_rows, 16)
            sp.dma_start(rows[8:56, :], conv_w[0].rearrange("j (t p) -> (j t) p", p=128)).then_inc(s_rows, 16)
            sp.dma_start(rows[56:57, :], gdn_norm_w).then_inc(s_rows, 16)
            sp.dma_start(rows[57:58, :], gla_norm_w).then_inc(s_rows, 16)
            sp.dma_start(rows[58:60, :], gla_gk_b[0].rearrange("(k p) -> k p", p=128)).then_inc(s_rows, 16)
            sp.dma_start(cst_rows, state_gdn_conv[0].rearrange("b w c -> (b w) c")).then_inc(s_rows, 16)
            for i in range(MIX):
                n = panels[i].shape[1]
                sp.dma_start(slot(i).rearrange("p (k n) -> p k n", k=n), panels[i]).then_inc(wfull[i], 16)
                if i == 0:
                    sp.dma_start(w_small[:, :, 0:8], win(C_AB, 8)).then_inc(s_small, 16)
                    sp.dma_start(w_small[:, :, 8:24], win(C_LR, 16)).then_inc(s_small, 16)
                    sp.dma_start(gk_up[:, :], gla_gk_up[0]).then_inc(s_small, 16)
                    sp.dma_start(hb[:, 0:4], dt_bias.to_broadcast([128, 4])).then_inc(s_misc, 16)
                    sp.dma_start(hb[:, 4:8], a_log.to_broadcast([128, 4])).then_inc(s_misc, 16)
            sp.dma_start(Sg[:, :, :], state_gdn[0].rearrange("b h d e -> d (b h) e")).then_inc(s_state, 16)
            sp.dma_start(Sl[:, :, :], state_gla[0].rearrange("b h d e -> (b h d) e")
                         .rearrange("(n p) e -> p n e", p=128)).then_inc(s_state, 16)
            sp.dma_start(wr[:, :, :], w_router[0].rearrange("(k p) e -> p k e", p=128)).then_inc(s_misc, 16)
            sp.dma_start(brt[:, :], b_router.to_broadcast([128, EXPERTS])).then_inc(s_misc, 16)
            for i in range(MIX, MIX_PANELS):
                if i == 24:
                    sp.wait_ge(o_ready, 2)
                    for c in range(MIX, RING):
                        sp.dma_start(chunk_dst(c), expert_chunk(0, c)).then_inc(wfull[c], 16)
                full(sp, last_use[i - MIX])
                n = panels[i].shape[1]
                sp.dma_start(slot(i % MIX).rearrange("p (k n) -> p k n", k=n), panels[i]).then_inc(wfull[i % MIX], 16)
            for c in range(MIX):
                full(sp, last_use[MIX_PANELS - MIX + c])
                sp.dma_start(chunk_dst(c), expert_chunk(0, c)).then_inc(wfull[c], 16)

            def load_expert(e, e_mod):
                for c in range(RING):
                    sp.wait_ge(wfree[c], e)
                    sp.dma_start(chunk_dst(c), expert_chunk(e_mod, c)).then_inc(wfull[c], 16)

            with sp.Fori(1, EXPERTS) as e:
                load_expert(e, e)
            sp.wait_ge(cnt_ready, 1)
            its = sp.value_load(nit[0:1, 1:2], min_val=EXPERTS, max_val=EXPERTS * ROUNDS)
            with sp.If(its > EXPERTS):
                with sp.Fori(EXPERTS, its) as e:
                    load_expert(e, e % EXPERTS)
            sp.wait_ge(fin_dve, 3)
            sp.dma_start(y_prompt[0].rearrange("(s p) d -> p s d", p=128), x_tm[:, 0:2, :]).then_inc(y_out, 16)
            sp.dma_start(y_sample.rearrange("b t d -> (b t) d"), x_tm[0:64, 2, :]).then_inc(y_out, 16)
            sp.wait_ge(out_sem, 16 * 6)
            sp.wait_ge(y_out, 32)

        @block.gpsimd
        def _(pool):
            step, _ = chain(pool, pool_c)

            def select(out, in_, pattern, base, mult, op=ALU.is_ge, fill=0.0):
                step(pool.affine_select(out=out, in_=in_, pattern=pattern, base=base, channel_multiplier=mult,
                                        compare_op=op, fill=fill))

            step(pool.memset(ident[:, :], 0.0))
            select(ident[:, :], ident[:, :], [[-1, 128]], 0, 1, ALU.not_equal, 1.0)
            step(pool.memset(ones[:, :], 1.0))
            step(pool.memset(eps[:, :], EPS), consts)
            select(triu[:, :], ones[:, :], [[1, 128]], 0, -1)
            for i, b in enumerate(LEVELS[1:]):
                v = blk[:, i, :].rearrange("p (n b) -> p n b", b=b)
                o = ones[:, :].rearrange("p (n b) -> p n b", b=b)
                select(v, o, [[-b, 128 // b], [0, b]], 0, 1)
                select(v, v, [[b, 128 // b], [0, b]], b - 1, -1)
            step(pool.tensor_tensor(tri8[:, :], triu[:, :], blk[:, 2, :], ALU.mult))
            step(pool.tensor_tensor(tri16[:, :], triu[:, :], blk[:, 3, :], ALU.mult))
            for i in range(7):
                big = blk[:, i, :] if i < 6 else ones[:, :]
                small = blk[:, i - 1, :] if i > 0 else ident[:, :]
                step(pool.tensor_tensor(lvm[i], big, small, ALU.subtract))
                step(pool.tensor_tensor(lvm[i], lvm[i], triu[:, :], ALU.mult))
            step(pool.tensor_copy(b8[:, :], blk[0:64, 2, 0:64]))
            step(pool.memset(bsel[:, :], 1.0))
            select(bsel[:, :], bsel[:, :], [[-8, 8]], 0, 1)
            select(bsel[:, :], bsel[:, :], [[8, 8]], 7, -1)
            step(pool.memset(rst[:, :], 1.0))
            step(pool.memset(rst[:, 0:256].rearrange("p (n b) -> p n b", b=128)[:, :, 0:1], 0.0))
            step(pool.memset(rst[:, 256:TOK].rearrange("p (n b) -> p n b", b=8)[:, :, 0:1], 0.0))
            step(pool.iota(iota[:, :], pattern=[[1, SLOTS]], base=0, channel_multiplier=0,
                           allow_small_or_imprecise_dtypes=True))
            step(pool.memset(ab[:, :, :], 0.0), consts)

            freed(pool, "tail2")
            pool.dma_start(conv_p[0, 0], tail_tm[0:3, :]).then_inc(out_sem, 16)
            pool.dma_start(conv_s[0].rearrange("b w c -> (b w) c"), tail_tm[3:27, :]).then_inc(out_sem, 16)
            pool.wait_ge(st_ready, 1)
            pool.dma_start(gdn_p[0, 0].rearrange("h d e -> d h e"), Sp[:, :, :]).then_inc(out_sem, 16)
            freed(pool, f"ss{HEADS - 1}1")
            pool.dma_start(gdn_s[0].rearrange("b h d e -> d (b h) e"), Sg[:, :, :]).then_inc(out_sem, 16)
            pool.wait_ge(out_sem, 64)
            pool.dma_start(x_tm[:, 0:2, :], x_prompt[0].rearrange("(s p) d -> p s d", p=128)).then_inc(s_x2, 16)
            pool.dma_start(x_tm[0:64, 2, :], x_sample.rearrange("b t d -> (b t) d")).then_inc(s_x2, 16)
            pool.dma_start(Sg[0:EXPERTS, 0:8, :], b_down[0].rearrange("e (a b) -> e a b", b=128)).then_inc(s_late, 16)
            pool.dma_start(Sg[:, 8:12, :], b_gate_up[0].rearrange("e (m j) -> (e m) j", j=128)
                           .rearrange("(g p) j -> p g j", p=128)).then_inc(s_late, 16)
            pool.wait_ge(st_ready, 2)
            pool.dma_start(gla_p[0, 0].rearrange("h d e -> (h d) e").rearrange("(n p) e -> p n e", p=128),
                           Slp[:, :, :]).then_inc(out_sem, 16)
            freed(pool, f"gss{HEADS - 1}1")
            pool.dma_start(gla_s[0].rearrange("b h d e -> (b h d) e").rearrange("(n p) e -> p n e", p=128),
                           Sl[:, :, :]).then_inc(out_sem, 16)
            full(pool, f"ub{KD - 1}")
            pool.dma_start(oAb[:, 0:D], norm2_w.to_broadcast([128, D])).then_inc(s_late, 16)
            pool.dma_start(oBb[:, 0:D], norm_f_w.rearrange("(a d) -> a d", a=1).to_broadcast([128, D])).then_inc(s_late, 16)

        xTe = flat(zgb, 0, (KD, 2 * SLOTS))
        pre = flat(zgb, 1024, (2, 512))
        y_sl = flat(hTb, 0, (D,))
        Psel = flat(hTb, 1024, (3, 2 * SLOTS))
        Gsel = flat(hTb, 1408, (3, 2 * SLOTS))
        GTs = flat(hTb, 1792, (TOK,))
        hm = [flat(zgb, 2048, (4, 2, SLOTS)), flat(cv[:, :, :].rearrange("p a b -> p (a b)"), 0, (4, 2, SLOTS))]
        gbuf = flat(qb, 0, (4, 2, SLOTS))
        ubuf = flat(kb, 0, (4, 2, SLOTS))
        sbuf_ = flat(Gc, 0, (4, 2, SLOTS))
        NCOL = ROUNDS * EXPERTS + 2
        vflat = vTM[:, :, :].rearrange("p a b -> p (a b)")
        slot_all = flat(vflat, 0, (3, NCOL))
        gate_all = flat(vflat, 3 * NCOL, (3, NCOL))
        h2 = flat(h2b, 0, (3, D))
        wT = flat(h2b, 3072, (TOK,))
        bdn = Sg[0:EXPERTS, 0:8, :].rearrange("e a b -> e (a b)")
        n2b, nfb = oAb[:, 0:D], oBb[:, 0:D]
        PRE, FMB, DN = (0, 1), (2, 3), (4, 5)

        @block.tensor
        def _(pe):
            seen = []

            def take(name):
                assert psum_order()[len(seen)] == name, (name, psum_order()[len(seen)])
                seen.append(name)
                b, u = PSUM_USE[name]
                if u:
                    pe.wait_ge(pfree[b], u)
                return bank[b]

            def done(ins, name):
                ins.then_inc(pfull[PSUM_USE[name][0]], 1)

            def panel(i, k):
                return slot(i % MIX).rearrange("p (k n) -> p k n", k=k)

            def panel_in(i):
                pe.wait_ge(wfull[i % MIX], 16 * (i // MIX + 1))

            def fm(name, i, c0, rhs, kk=KD, m=128, k_of=None):
                o = take(name)
                w = panel(i, kk)
                for k in range(kk):
                    mm = pe.matmul(o[0:m, 0:TOK], w[:, k, c0:c0 + m], rhs[:, k, :], start=(k == 0), stop=(k == kk - 1))
                return mm

            pe.wait_ge(consts, 2)
            pe.wait_ge(s_rows, 16 * 6)
            o = take("cols")
            done(pe.transpose(o[:, 0:60], rows[0:60, :], ident[0:60, 0:60]), "cols")
            o = take("cst")
            for t in range(QT):
                mm = pe.transpose(o[:, 24 * t:24 * t + 24], cst_rows[:, 128 * t:128 * t + 128], ident[0:24, 0:24])
            done(mm, "cst")
            for s in range(3):
                n = TILE_N[s]
                pe.wait_ge(xs_ready, s + 1)
                for f in range(2):
                    o = take(f"xT{s}{f}")
                    for k in range(4):
                        mm = pe.transpose(o[:, 128 * k:128 * k + n], x_tm[0:n, s, 512 * f + 128 * k:512 * f + 128 * k + 128],
                                          ident[0:n, 0:n])
                    done(mm, f"xT{s}{f}")
            freed(pe, "xT21")
            for t in range(QT):
                panel_in(t // 2)
                done(fm(f"qkv{t}", t // 2, 128 * (t % 2), hT), f"qkv{t}")
            pe.wait_ge(s_small, 48)
            o = take("ab")
            for s in range(3):
                n = TILE_N[s]
                for k in range(KD):
                    mm = pe.matmul(o[0:n, 8 * s:8 * s + 8], hT[:, k, TILE_0[s]:TILE_0[s] + n], w_small[:, k, 0:8],
                                   start=(k == 0), stop=(k == KD - 1))
            done(mm, "ab")
            o = take("lr")
            for k in range(KD):
                mm = pe.matmul(o[0:RANK, 0:TOK], w_small[:, k, 8:24], hT[:, k, :], start=(k == 0), stop=(k == KD - 1))
            done(mm, "lr")

            for t in range(4):
                panel_in(P_Z + t // 2)
                done(fm(f"z{t}", P_Z + t // 2, 128 * (t % 2), hT), f"z{t}")
            for nm, p in (("qb", P_QB), ("kb", P_KB)):
                panel_in(p)
                for t in range(2):
                    done(fm(f"{nm}{t}", p, 128 * t, hT), f"{nm}{t}")
            freed(pe, "lr")
            for t in range(2):
                o = take(f"gk{t}")
                done(pe.matmul(o[:, 0:TOK], gk_up[:, 128 * t:128 * t + 128], lrT[:, :], start=True, stop=True), f"gk{t}")
            pe.wait_ge(tails_ready, 1)
            for g in range(3):
                o = take(f"tail{g}")
                for t in range(4):
                    mm = pe.transpose(o[0:27, 128 * t:128 * t + 128], tails[:, 4 * g + t, :], ident[:, :])
                done(mm, f"tail{g}")
            panel_in(P_VB)
            panel_in(P_VB + 1)
            for s in range(3):
                n = TILE_N[s]
                o = take(f"vb{s}")
                for f in range(2):
                    for k in range(KD):
                        mm = pe.matmul(o[0:n, 256 * f:256 * f + 256], hT[:, k, TILE_0[s]:TILE_0[s] + n],
                                       panel(P_VB + f, KD)[:, k, :], start=(k == 0), stop=(k == KD - 1))
                done(mm, f"vb{s}")
            for t in range(4):
                panel_in(P_GB + t // 2)
                done(fm(f"g{t}", P_GB + t // 2, 128 * (t % 2), hT), f"g{t}")

            for t in range(8):
                pe.wait_ge(sq_ready, t + 1)
                o = take(f"nrm{t}")
                src = (oA if t < 4 else oB)[:, t % 4, :]
                done(pe.matmul(o[:, 0:TOK], ones[:, :], src, start=True, stop=True), f"nrm{t}")
            pe.wait_ge(g_ready, 1)
            o = take("gc")
            for s in range(3):
                n = TILE_N[s]
                tri = triu if s < 2 else tri8
                mm = pe.matmul(o[0:n, 8 * s:8 * s + 4], tri[0:n, 0:n], g_tm[0:n, s, :], start=True, stop=True)
                lhs = ones[0:n, 0:n] if s < 2 else b8[0:n, 0:n]
                mm = pe.matmul(o[0:n, 8 * s + 4:8 * s + 8], lhs, g_tm[0:n, s, :], start=True, stop=True)
            done(mm, "gc")
            for h in range(HEADS):
                for nm, col in (("gB", g_tm), ("bB", beta)):
                    o = take(f"{nm}{h}")
                    for s in range(3):
                        n = TILE_N[s]
                        rhs = ident if nm == "bB" else (triu if s < 2 else tri8)
                        mm = pe.matmul(o[:, TILE_0[s]:TILE_0[s] + n], col[0:n, s, h:h + 1].to_broadcast([n, 128]),
                                       rhs[0:n, 0:n], start=True, stop=True)
                    done(mm, f"{nm}{h}")
            pe.wait_ge(qk_ready, 8)
            for s in range(3):
                n = TILE_N[s]
                o = p3(take(f"kT{s}"), HEADS, 128)
                for h in range(HEADS):
                    mm = pe.transpose(o[0:n, h, :], qkv[:, 4 + h, TILE_0[s]:TILE_0[s] + n], ident[:, :])
                done(mm, f"kT{s}")
            pe.wait_ge(kb_ready, HEADS)
            for s in range(3):
                n, a = TILE_N[s], TILE_0[s]
                for nm in "AQ":
                    o = p3(take(f"{nm}{s}"), HEADS, 128)
                    for h in range(HEADS):
                        rhs = oA[:, h, a:a + n] if nm == "A" else qkv[:, h, a:a + n]
                        mm = pe.matmul(o[0:n, h, 0:n], qkv[:, 4 + h, a:a + n], rhs, start=True, stop=True)
                    done(mm, f"{nm}{s}")
            for s in range(3):
                n = TILE_N[s]
                pe.wait_ge(t2t_ready, s + 1)
                o = p3(take(f"t2{s}"), HEADS, 128)
                for h in range(HEADS):
                    mm = pe.transpose(o[0:n, h, 0:n], TT[0:n, s, h, 0:n], ident[0:n, 0:n])
                done(mm, f"t2{s}")
            lts = 0
            invs = [0, 0, 0]
            for b in LEVELS[1:]:
                tiles = [s for s in range(3) if b in levels_of(s)]
                for s in tiles:
                    n = TILE_N[s]
                    lts += 1
                    pe.wait_ge(lt_ready, lts)
                    if b == 2:
                        freed(pe, f"t2{s}")
                    else:
                        freed(pe, f"Z{s}{b // 2}")
                    o = p3(take(f"X{s}{b}"), HEADS, 128)
                    for h in range(HEADS):
                        mm = pe.matmul(o[0:n, h, 0:n], LT[0:n, s, h, 0:n], T_[0:n, s, h, 0:n], start=True, stop=True)
                    done(mm, f"X{s}{b}")
                for s in tiles:
                    n = TILE_N[s]
                    freed(pe, f"X{s}{b}")
                    if b != levels_of(s)[-1]:
                        o = p3(take(f"Y{s}{b}"), HEADS, 128)
                        for h in range(HEADS):
                            mm = pe.matmul(o[0:n, h, 0:n], TT[0:n, s, h, 0:n], X1[0:n, s, h, 0:n], start=True, stop=True)
                        done(mm, f"Y{s}{b}")
                    o = p3(take(f"Z{s}{b}"), HEADS, 128)
                    for h in range(HEADS):
                        mm = pe.matmul(o[0:n, h, 0:n], X1[0:n, s, h, 0:n], TT[0:n, s, h, 0:n], start=True, stop=True)
                    done(mm, f"Z{s}{b}")

            def turn_rhs(s, src, off):
                n = TILE_N[s]
                o = p3(take(f"rt{s}"), HEADS, 128)
                for h in range(HEADS):
                    mm = pe.transpose(o[0:n, h, :], src[:, h, off:off + n], ident[:, :])
                done(mm, f"rt{s}")
                freed(pe, f"rt{s}")
                freed(pe, f"Z{s}{levels_of(s)[-1]}")
                o = p3(take(f"v{s}"), HEADS, 128)
                for h in range(HEADS):
                    mm = pe.matmul(o[0:n, h, :], TT[0:n, s, h, 0:n], R[0:n, s, h, :], start=True, stop=True)
                done(mm, f"v{s}")
                freed(pe, f"v{s}")
                o = p3(take(f"o{s}"), HEADS, 128)
                for h in range(HEADS):
                    mm = pe.matmul(o[:, h, 0:n], R[0:n, s, h, :], attnT[0:n, s, h, 0:n], start=True, stop=(s != 1))
                    if s == 1:
                        mm = pe.matmul(o[:, h, 0:n], Sp[:, h, :], kbqg[:, 1, h, 128:256], start=False, stop=True)
                done(mm, f"o{s}")

            def new_state(s):
                n = TILE_N[s]
                o = p3(take(f"s{s}"), HEADS, 128)
                for h in range(HEADS):
                    mm = pe.matmul(o[:, h, :], kdT[0:n, s, h, :], R[0:n, s, h, :], start=True, stop=True)
                done(mm, f"s{s}")

            turn_rhs(0, qkv[:, 8:12, :], 0)
            new_state(0)
            freed(pe, "s0")
            o = p3(take("ks1"), HEADS, 128)
            for h in range(HEADS):
                mm = pe.matmul(o[:, h, :], Sp[:, h, :], kbqg[:, 0, h, 128:256], start=True, stop=True)
            done(mm, "ks1")
            freed(pe, "ks1")
            turn_rhs(1, LT[:, 1, :, :], 0)
            new_state(1)
            pe.wait_ge(s_state, 32)
            o = take("ks2")[:, :].rearrange("p (h z t) -> p h z t", h=HEADS, z=2)
            for h in range(HEADS):
                for b in range(BATCHES):
                    mm = pe.matmul(o[:, h, :, 8 * b:8 * b + 8], Sg[:, HEADS * b + h, :],
                                   kbqg[:, :, h, PROMPT + 8 * b:PROMPT + 8 * b + 8], start=True, stop=True)
            done(mm, "ks2")
            freed(pe, "ks2")
            turn_rhs(2, LT[:, 2, :, :], 0)
            for h in range(HEADS):
                for f in range(2):
                    pe.wait_ge(vm_ready, h + 1)
                    o = take(f"ss{h}{f}")
                    done(pe.matmul(o[:, :], kdT[0:64, 2, h, :], VM[0:64, 4 * f:4 * f + 4, :], start=True, stop=True),
                         f"ss{h}{f}")
            for h in range(HEADS):
                pe.wait_ge(osq_ready, h + 1)
                o = take(f"on{h}")
                done(pe.matmul(o[:, 0:TOK], ones[:, :], oB[:, h, :], start=True, stop=True), f"on{h}")

            for lv in range(4):
                pe.wait_ge(lev_ready, lv + 1)
                for s in range(3 if lv == 0 else 2):
                    n, a = TILE_N[s], TILE_0[s]
                    for r in range(2):
                        o = p3(take(f"L{lv}{s}{r}"), 2, 128)
                        for hp in range(2):
                            mm = pe.matmul(o[0:n, hp, 0:n], kt[64 * r:64 * r + 64, lv % 2, hp, a:a + n],
                                           qt[64 * r:64 * r + 64, lv % 2, hp, a:a + n], start=True, stop=True)
                        done(mm, f"L{lv}{s}{r}")
            pe.wait_ge(kd_ready, 1)
            for s in range(3):
                n, a = TILE_N[s], TILE_0[s]
                o = p3(take(f"gT{s}"), 2, 128)
                for hp in range(2):
                    mm = pe.transpose(o[0:n, hp, :], kdF[:, hp, a:a + n], ident[:, :])
                done(mm, f"gT{s}")
            for s in range(3):
                n, a = TILE_N[s], TILE_0[s]
                pe.wait_ge(at_ready, min(s + 1, 2))
                if s == 1:
                    freed(pe, "gs0")
                for r in range(2):
                    o = p3(take(f"ob{s}{r}"), 2, 128)
                    for hp in range(2):
                        h = 2 * hp + r
                        mm = pe.matmul(o[:, hp, 0:n], vTM[:, s, 128 * h:128 * h + 128], AT[:, s, h, 0:n],
                                       start=True, stop=(s != 1), skip_group_check=(s == 2))
                        if s == 1:
                            mm = pe.matmul(o[:, hp, 0:n], Slp[64 * r:64 * r + 64, hp, :],
                                           qG[64 * r:64 * r + 64, hp, a:a + n], start=False, stop=True)
                        if s == 2:
                            for b in range(BATCHES):
                                mm = pe.matmul(o[:, hp, 8 * b:8 * b + 8], Sl[64 * r:64 * r + 64, 2 * b + hp, :],
                                               qG[64 * r:64 * r + 64, hp, a + 8 * b:a + 8 * b + 8], start=False,
                                               stop=True, skip_group_check=True)
                    done(mm, f"ob{s}{r}")
                if s < 2:
                    freed(pe, f"gT{s}")
                    o = p3(take(f"gs{s}"), 2, 256)
                    for hp in range(2):
                        mm = pe.matmul(o[:, hp, :], kdG[0:n, s, hp, :], vTM[0:n, s, 256 * hp:256 * hp + 256],
                                       start=True, stop=True)
                    done(mm, f"gs{s}")
            freed(pe, "gT2")
            for h in range(HEADS):
                r = 64 * (h % 2)
                for f in range(2):
                    pe.wait_ge(vm_ready, HEADS + h + 1)
                    o = take(f"gss{h}{f}")
                    done(pe.matmul(o[r:r + 64, :], kdG[0:64, 2, h // 2, r:r + 64], VM[0:64, 4 * f:4 * f + 4, :],
                                   start=True, stop=True), f"gss{h}{f}")
            for h in range(HEADS):
                pe.wait_ge(osq_ready, HEADS + h + 1)
                o = take(f"om{h}")
                done(pe.matmul(o[:, 0:TOK], ones[:, :], osq[:, h, :], start=True, stop=True), f"om{h}")

            for m in range(KD):
                f, i = m // 4, (m % 4) // 2
                p = P_M + 6 * f
                for nm, q in (("ga", p + 2 + 2 * i), ("gb", p + 3 + 2 * i)):
                    panel_in(q)
                    done(fm(f"{nm}{m}", q, 128 * (m % 2), hT), f"{nm}{m}")
                if m == 0:
                    pe.wait_ge(o_ready, 2)
                for nm, q, src in (("ua", p, oA), ("ub", p + 1, oB)):
                    panel_in(q)
                    done(fm(f"{nm}{m}", q, 128 * (m % 4), src, HEADS), f"{nm}{m}")
            pe.wait_ge(mrg_ready, KD)
            for i in range(4):
                panel_in(P_O + i)
            for s in range(3):
                n, a = TILE_N[s], TILE_0[s]
                for f in range(2):
                    o = take(f"wo{s}{f}")
                    for k in range(KD):
                        mm = pe.matmul(o[0:n, :], merged[:, k, a:a + n], panel(P_O + k // 2, 2)[:, k % 2, 512 * f:512 * f + 512],
                                       start=(k == 0), stop=(k == KD - 1))
                    done(mm, f"wo{s}{f}")

            for s in range(3):
                n, a = TILE_N[s], TILE_0[s]
                pe.wait_ge(h2_ready, s + 1)
                for f in range(2):
                    o = p3(take(f"hT{s}{f}"), 4, 128)
                    for k in range(4):
                        mm = pe.transpose(o[:, k, 0:n], h2[0:n, s, 512 * f + 128 * k:512 * f + 128 * k + 128],
                                          ident[0:n, 0:n])
                    done(mm, f"hT{s}{f}")
            pe.wait_ge(s_misc, 64)
            for s in range(3):
                n, a = TILE_N[s], TILE_0[s]
                freed(pe, f"hT{s}1")
                freed(pe, f"hT{s}0")
                o = take(f"lg{s}")
                for k in range(KD):
                    mm = pe.matmul(o[0:n, 0:EXPERTS], hT[:, k, a:a + n], wr[:, k, :], start=(k == 0), stop=(k == KD - 1))
                done(mm, f"lg{s}")
            pe.wait_ge(gate_ready, 1)
            for s in range(3):
                n = TILE_N[s]
                o = take(f"sl{s}")
                for q in range(s):
                    pe.matmul(o[0:n, 0:EXPERTS], ones[0:TILE_N[q], 0:n], msk[0:TILE_N[q], q, :], start=(q == 0), stop=False)
                done(pe.matmul(o[0:n, 0:EXPERTS], triu[0:n, 0:n], msk[0:n, s, :], start=(s == 0), stop=True), f"sl{s}")
            o = take("cnt")
            for s in range(3):
                mm = pe.matmul(o[:, 0:EXPERTS], ones[0:TILE_N[s], :], msk[0:TILE_N[s], s, :], start=(s == 0), stop=(s == 2))
            done(mm, "cnt")
            o = take("wT")
            for s in range(3):
                n, a = TILE_N[s], TILE_0[s]
                mm = pe.transpose(o[0:EXPERTS, a:a + n], gate_all[0:n, s, 0:EXPERTS], ident[0:n, 0:n])
            done(mm, "wT")
            pe.wait_ge(s_late, 64)
            o = take("bgu")
            for g in range(4):
                mm = pe.transpose(o[:, 128 * g:128 * g + 128], Sg[:, 8 + g, :], ident[:, :])
            done(mm, "bgu")
            freed(pe, "wT")
            for s in range(3):
                n, a = TILE_N[s], TILE_0[s]
                for f in range(2):
                    o = take(f"bd{s}{f}")
                    done(pe.matmul(o[0:n, :], wT[0:EXPERTS, a:a + n], bdn[:, 512 * f:512 * f + 512], start=True, stop=True),
                         f"bd{s}{f}")
            assert len(seen) == len(psum_order())

            for b in range(8):
                pe.wait_ge(pfree[b], max(u for bb, u in PSUM_USE.values() if bb == b) + 1)
            pe.wait_ge(cnt_ready, 1)
            its = pe.value_load(nit[0:1, 0:1], min_val=PAIRS, max_val=PAIRS * ROUNDS)

            def gather(fs=(0, 1)):
                for f in fs:
                    o = p3(bank[7 - f], 4, 2 * SLOTS)
                    for k in range(4):
                        c = 512 * f + 128 * k
                        for s in range(3):
                            mm = pe.matmul(o[:, k, :], h2[0:TILE_N[s], s, c:c + 128], Psel[0:TILE_N[s], s, :],
                                           start=(s == 0), stop=(s == 2))
                    mm.then_inc(m_full[7 - f], 1)

            def turn_gates():
                for s in range(3):
                    n, a = TILE_N[s], TILE_0[s]
                    mm = pe.transpose(bank[7][:, a:a + n], Gsel[0:n, s, :], ident[0:n, 0:n])
                mm.then_inc(m_full[7], 1)

            def scatter(j0, acc0):
                for j in range(j0, j0 + 3):
                    s, f = j // 2, j % 2
                    n, a = TILE_N[s], TILE_0[s]
                    if j >= 2:
                        pe.wait_ge(acc_done, acc0 + j - 1)
                    pe.matmul(bank[7 - j % 2][0:n, :], GTs[:, a:a + n], y_sl[:, 512 * f:512 * f + 512], start=True,
                              stop=True).then_inc(m_full[7 - j % 2], 1)

            def halves(o, lhs, w, start, stop):
                for f in range(2):
                    mm = pe.matmul(o[64 * f:64 * f + 64, :], lhs, w[:, 512 * f:512 * f + 512], start=start, stop=stop)
                return mm

            def gate_up(x, e):
                for c in range(KD):
                    pe.wait_ge(wfull[c], e * 16 + 16 * (1 + (MIX_USES if c < MIX else 0)))
                    for q in range(2):
                        mm = halves(bank[PRE[q]], xTe[:, c, SLOTS * x:SLOTS * x + SLOTS],
                                    slot(c)[:, FF * q:FF * q + FF], c == 0, c == KD - 1)
                    mm.then_inc(wfree[c], 1)

            def turn_pre():
                for q in range(2):
                    for j in range(4):
                        mm = pe.transpose(bank[FMB[q]][:, 128 * j:128 * j + 128], pre[:, q, 128 * j:128 * j + 128],
                                          ident[:, :])
                mm.then_inc(t_full, 1)

            def down(x, e):
                for c in range(KD, RING):
                    pe.wait_ge(wfull[c], e * 16 + 16)
                    for i in range(2):
                        k = 2 * (c - KD) + i
                        mm = halves(bank[DN[x]], hm[x][:, k % 4, k // 4, :], slot(c)[:, D * i:D * i + D], k == 0,
                                    k == FT - 1)
                    mm.then_inc(wfree[c], 1)

            pe.wait_ge(p_ready, 1)
            gather()
            with pe.Fori(0, its) as n:
                pe.wait_ge(xg_done, n * 2 + 2)
                gate_up(0, n * 2)
                pe.wait_ge(yt_done, n * 2 + 1)
                pe.wait_ge(gtr_done, n + 1)
                scatter(0, n * 6)
                pe.wait_ge(pre_done, n * 2 + 1)
                turn_pre()
                scatter(3, n * 6)
                pe.wait_ge(hm_ready, n * 2 + 1)
                down(0, n * 2)
                gate_up(1, n * 2 + 1)
                pe.wait_ge(p_ready, n + 2)
                pe.wait_ge(acc_done, n * 6 + 5)
                gather((0,))
                pe.wait_ge(pre_done, n * 2 + 2)
                turn_pre()
                pe.wait_ge(acc_done, n * 6 + 6)
                gather((1,))
                pe.wait_ge(xg_done, n * 2 + 3)
                pe.wait_ge(gm_ready, n + 1)
                turn_gates()
                pe.wait_ge(hm_ready, n * 2 + 2)
                down(1, n * 2 + 1)
            pe.wait_ge(xg_done, its * 2 + 2)
            pe.wait_ge(yt_done, its * 2 + 1)
            pe.wait_ge(gtr_done, its + 1)
            scatter(0, its * 6)
            scatter(3, its * 6)

        def b6(n, i):
            return n * 4 + (2 + i)

        def b7(n, i):
            return n * 5 + (2 + i)

        def rms_act(step, src, n, acc, signal, scratch, width=D):
            step(nc.scalar.activation(scratch, src, ACT.Square, accum_out=ss[0:n, acc:acc + 1]))
            step(nc.scalar.activation(rs[0:n, acc:acc + 1], ss[0:n, acc:acc + 1], ACT.Ln, scale=1.0 / width,
                                      bias=eps[0:n, :]))
            step(nc.scalar.activation(rs[0:n, acc:acc + 1], rs[0:n, acc:acc + 1], ACT.Exp, scale=-0.5), signal)

        @block.scalar
        def _(act):
            step, free = chain(act, act_c)
            A = nc.scalar.activation

            def inv_root(name, dst, width, signal):
                o = full(act, name)
                free(A(dst, o[:, 0:TOK], ACT.Ln, scale=1.0 / width, bias=eps[:, :]), name)
                step(A(dst, dst, ACT.Exp, scale=-0.5), signal)

            act.wait_ge(consts, 2)
            act.wait_ge(s_x, 32)
            for s in range(3):
                n = TILE_N[s]
                rms_act(step, x_tm[0:n, s, :], n, s, rs_ready, h2b[0:n, 0:D])
            def silu_conv(t):
                act.wait_ge(conv_done, t + 1)
                step(A(qkv[:, t, 0:PROMPT], cv[:, t % 2, 0:PROMPT], ACT.Silu))
                v = cv[:, t % 2, CATS:CATN].rearrange("p (b w) -> p b w", w=3 + STEPS)[:, :, 0:STEPS]
                step(A(qkv[:, t, PROMPT:TOK].rearrange("p (b w) -> p b w", w=STEPS), v, ACT.Silu), silu_done)

            for t in range(QT):
                o = full(act, f"qkv{t}")
                step(nc.scalar.copy(cat[:, t, 3:CATS], o[:, 0:PROMPT]))
                v = cat[:, t, CATS:CATN].rearrange("p (b w) -> p b w", w=3 + STEPS)[:, :, 3:]
                free(nc.scalar.copy(v, o[:, PROMPT:TOK].rearrange("p (b w) -> p b w", w=STEPS)), f"qkv{t}")
                if t >= 2:
                    silu_conv(t - 2)
            silu_conv(QT - 2)
            silu_conv(QT - 1)
            o = full(act, "lr")
            free(nc.scalar.copy(lrT[:, :], o[0:RANK, 0:TOK]), "lr")
            for t in range(4):
                o = full(act, f"z{t}")
                free(A(zg[:, t, :], o[:, 0:TOK], ACT.Silu), f"z{t}")
            for t in range(2):
                o = full(act, f"qb{t}")
                free(nc.scalar.mul(qb3[:, t, :], o[:, 0:TOK], DK_B ** -0.5), f"qb{t}")
            for t in range(2):
                o = full(act, f"kb{t}")
                free(nc.scalar.copy(kb3[:, t, :], o[:, 0:TOK]), f"kb{t}")
            freed(act, "cols")
            for t in range(2):
                o = full(act, f"gk{t}")
                free(A(G3[:, t, :], o[:, 0:TOK], ACT.Identity, bias=cols[:, 58 + t:59 + t]), f"gk{t}")
            for g in range(3):
                o = full(act, f"tail{g}")
                free(nc.scalar.copy(tail_tm[0:27, 512 * g:512 * g + 512], o[0:27, :]), f"tail{g}")
            for s in range(3):
                n = TILE_N[s]
                o = full(act, f"vb{s}")
                free(nc.scalar.copy(vTM[0:n, s, :], o[0:n, :]), f"vb{s}")
            for t in range(4):
                o = full(act, f"g{t}")
                free(A(zg[:, 4 + t, :], o[:, 0:TOK], ACT.Silu), f"g{t}")

            for t in range(8):
                dst = (oA if t < 4 else oB)[:, t % 4, :]
                step(A(dst, qkv[:, t, :], ACT.Square), sq_ready)
            act.wait_ge(ab_mid, 1)
            step(A(soft[:, :, :], absu[:, :, :], ACT.Exp, scale=-1.0))
            step(A(soft[:, :, :], soft[:, :, :], ACT.Ln, bias=ones[:, 0:1]))
            step(A(beta[:, :, :], ab[:, :, 4:8], ACT.Exp, scale=-1.0))
            act.wait_ge(s_misc, 64)
            step(A(hb[:, 4:8], hb[:, 4:8], ACT.Exp), ab_exp)
            for t in range(8):
                inv_root(f"nrm{t}", (oA if t < 4 else oB)[:, t % 4, :], 1.0, nrm_ready)
            freed(act, "gc")
            step(A(kdf[:, :, :], kdf[:, :, :], ACT.Exp))
            step(A(glp[:, :, :], glp[:, :, :], ACT.Exp), kdf_ready)
            for h in range(HEADS):
                o = full(act, f"gB{h}")
                for s in range(3):
                    n, a = TILE_N[s], TILE_0[s]
                    step(A(attnT[0:n, s, h, 0:n], o[0:n, a:a + n], ACT.Exp, bias=gneg[0:n, s, h:h + 1]))
                free(A(kbqg[:, 0, h, :], o[:, 0:TOK], ACT.Exp), f"gB{h}")

            def evac(name, dst, n, w=128):
                o = p3(full(act, name), HEADS, 128)
                free(nc.scalar.copy(dst, o[0:n, :, 0:w]), name)

            for s in range(3):
                n = TILE_N[s]
                evac(f"t2{s}", T_[0:n, s, :, 0:n], n, n)
            for b in LEVELS[1:]:
                for s in range(3):
                    if b in levels_of(s):
                        n = TILE_N[s]
                        evac(f"X{s}{b}", X1[0:n, s, :, 0:n], n, n)
            for s in range(3):
                n, a = TILE_N[s], TILE_0[s]
                evac(f"rt{s}", R[0:n, s, :, :], n)
                evac(f"v{s}", R[0:n, s, :, :], n)
                if s < 2:
                    evac(f"o{s}", oA[:, :, a:a + n], 128, n)
                if s == 0:
                    evac("s0", Sp[:, :, :], 128)
            freed(act, "o2")
            for h in range(HEADS):
                step(A(oB[:, h, :], oA[:, h, :], ACT.Square), osq_ready)
            for h in range(HEADS):
                inv_root(f"on{h}", oB[:, h, :], DV, onr_ready)

            step(A(ek[:, :, :], G3[:, :, :], ACT.Abs))
            step(A(ek[:, :, :], ek[:, :, :], ACT.Exp, scale=-1.0))
            step(A(ek[:, :, :], ek[:, :, :], ACT.Ln, bias=ones[:, 0:1]), la_act)
            for lv in range(4):
                w = TOK if lv == 0 else PROMPT
                act.wait_ge(lev_sub, lv + 1)
                step(A(eq[:, :, 0:w], eq[:, :, 0:w], ACT.Exp))
                step(A(ek[:, :, 0:w], ek[:, :, 0:w], ACT.Exp), lev_exp)
            act.wait_ge(lev_sub, 5)
            step(A(eq[:, :, :], G3[:, :, :], ACT.Exp))
            step(A(ek[:, :, :], ek[:, :, :], ACT.Exp), lev_exp)
            for s in range(3):
                n = TILE_N[s]
                o = p3(full(act, f"gT{s}"), 2, 128)
                free(nc.scalar.copy(kdG[0:n, s, :, :], o[0:n, :, :]), f"gT{s}")
            act.wait_ge(o_ready, 1)
            oB_r = oB.rearrange("p (a r) t -> p r a t", r=2)
            for s in range(3):
                n, a = TILE_N[s], TILE_0[s]
                for r in range(2):
                    o = p3(full(act, f"ob{s}{r}"), 2, 128)
                    free(nc.scalar.copy(oB_r[:, r, :, a:a + n], o[:, :, 0:n]), f"ob{s}{r}")
                if s == 0:
                    o = p3(full(act, "gs0"), 2, 256)
                    step(nc.scalar.copy(Slp[0:64, :, :], o[0:64, :, 0:128]))
                    free(nc.scalar.copy(Slp[64:128, :, :], o[64:128, :, 128:256]), "gs0")
            for h in range(HEADS):
                step(A(osq[:, h, :], oB[:, h, :], ACT.Square), osq_ready)
            for h in range(HEADS):
                inv_root(f"om{h}", osq[:, h, :], DV, onr_ready)

            act.wait_ge(o_ready, 2)
            for m in range(KD):
                if m >= 2:
                    act.wait_ge(mrg_ready, m - 1)
                o = full(act, f"ga{m}")
                free(A(qb3[:, m % 2, :], o[:, 0:TOK], ACT.Sigmoid), f"ga{m}")
                o = full(act, f"gb{m}")
                free(A(kb3[:, m % 2, :], o[:, 0:TOK], ACT.Sigmoid), f"gb{m}")
            for s in range(3):
                n = TILE_N[s]
                freed(act, f"wo{s}0")
                freed(act, f"wo{s}1")
                rms_act(step, x_tm[0:n, s, :], n, 3 + s, x2_rs, zgb[0:n, 0:D])
            for s in range(3):
                n, a = TILE_N[s], TILE_0[s]
                for f in range(2):
                    o = p3(full(act, f"hT{s}{f}"), 4, 128)
                    free(nc.scalar.copy(hT[:, 4 * f:4 * f + 4, a:a + n], o[:, :, 0:n]), f"hT{s}{f}")
            for s in range(3):
                n = TILE_N[s]
                act.wait_ge(route_max, s + 1)
                step(A(rg4[0:n, s, :], rt8[0:n, s, 0:TOP], ACT.Exp, bias=rneg[0:n, s, 0:1],
                       accum_out=rneg[0:n, s, 1:2]), route_exp)
            o = full(act, "wT")
            free(nc.scalar.copy(wT[0:EXPERTS, :], o[0:EXPERTS, 0:TOK]), "wT")

            o = full(act, "bgu")
            free(nc.scalar.copy(bcol[:, :], o[:, :]), "bgu")

            def link(ins, s, value):
                ins.then_inc(s, 1)
                act.wait_ge(s, value)

            def take_tokens(f, value, done):
                b = 7 - f
                act.wait_ge(m_full[b], value)
                link(nc.scalar.copy(xTe[:, 4 * f:4 * f + 4, :], p3(bank[b], 4, 128)), xg_done, done)

            def take_pre(x, n):
                act.wait_ge(wfree[KD - 1], n * 2 + (x + 1))
                link(nc.scalar.copy(pre[:, 0, :], bank[PRE[0]][:, :]), m_act, n * 4 + (2 * x + 1))
                link(nc.scalar.copy(pre[:, 1, :], bank[PRE[1]][:, :]), pre_done, n * 2 + (x + 1))

            def sigmoid(x, n):
                act.wait_ge(pre_sig, n * 2 + (x + 1))
                link(A(sbuf_[:, :, :, :], gbuf[:, :, :, :], ACT.Sigmoid, scale=ALPHA), sg_ready, n * 2 + (x + 1))

            def take_y(x, n):
                act.wait_ge(wfree[RING - 1], n * 2 + (x + 1))
                for f in range(2):
                    ins = nc.scalar.copy(y_sl[SLOTS * x:SLOTS * x + SLOTS, 512 * f:512 * f + 512],
                                         bank[DN[x]][64 * f:64 * f + 64, :])
                    if f == 0:
                        link(ins, m_act, n * 4 + (2 * x + 2))
                    else:
                        link(ins, yt_done, n * 2 + (x + 2))

            act.wait_ge(cnt_ready, 1)
            its = act.value_load(nit[0:1, 0:1], min_val=PAIRS, max_val=PAIRS * ROUNDS)
            take_tokens(0, 1, 1)
            take_tokens(1, 1, 2)
            with act.Fori(0, its) as n:
                take_pre(0, n)
                sigmoid(0, n)
                take_y(0, n)
                take_pre(1, n)
                take_tokens(0, b7(n, 3), n * 2 + 3)
                sigmoid(1, n)
                take_tokens(1, b6(n, 3), n * 2 + 4)
                act.wait_ge(m_full[7], b7(n, 4))
                link(nc.scalar.copy(GTs[:, :], bank[7][:, 0:TOK]), gtr_done, n + 2)
                take_y(1, n)
            act.wait_ge(acc_done, its * 6 + 6)
            for s in range(3):
                n = TILE_N[s]
                rms_act(step, x_tm[0:n, s, :], n, s, fin_act, zgb[0:n, 0:D])

        @block.vector
        def _(dve):
            step, free = chain(dve, dve_c)
            V = nc.vector
            TTo, TS, STT = V.tensor_tensor, V.tensor_scalar, V.scalar_tensor_tensor

            step(V.memset(kdf[:, :, :], 0.0))
            o = full(dve, "cols")
            free(V.tensor_copy(cols[:, 0:60], o[:, 0:60]), "cols")
            step(V.memset(cat[:, :, 0:3], 0.0))
            o = full(dve, "cst")
            v = cat[:, :, CATS:CATN].rearrange("p t (b w) -> p t b w", w=3 + STEPS)[:, :, :, 0:3]
            free(V.tensor_copy(v, o[:, 0:24 * QT].rearrange("p (t b w) -> p t b w", t=QT, w=3)), "cst")
            for s in range(3):
                n = TILE_N[s]
                dve.wait_ge(rs_ready, s + 1)
                step(TS(x_tm[0:n, s, :], x_tm[0:n, s, :], rs[0:n, s:s + 1], None, ALU.mult), xs_ready)
            for s in range(3):
                n, a = TILE_N[s], TILE_0[s]
                for f in range(2):
                    o = p3(full(dve, f"xT{s}{f}"), 4, 128)
                    free(TTo(hT[:, 4 * f:4 * f + 4, a:a + n], o[:, :, 0:n], last(cols[:, 4 * f:4 * f + 4], n), ALU.mult),
                         f"xT{s}{f}")
            for t in range(QT):
                freed(dve, f"qkv{t}")
                if t >= 2:
                    dve.wait_ge(silu_done, t - 1)
                c = cv[:, t % 2, 0:CONVN]
                step(TS(c, cat[:, t, 0:CONVN], cols[:, 8 + t:9 + t], None, ALU.mult))
                for j in range(1, 4):
                    step(STT(out=c, in0=cat[:, t, j:j + CONVN], scalar=cols[:, 8 + QT * j + t:9 + QT * j + t], in1=c,
                             op0=ALU.mult, op1=ALU.add), conv_done if j == 3 else None)
            step(V.tensor_copy(tails[:, :, 0:3], cat[:, :, PROMPT:PROMPT + 3]))
            v = cat[:, :, CATS:CATN].rearrange("p t (b w) -> p t b w", w=3 + STEPS)[:, :, :, STEPS:]
            step(V.tensor_copy(tails[:, :, 3:27].rearrange("p t (b w) -> p t b w", w=3), v), tails_ready)

            dve.wait_ge(consts, 2)
            o = full(dve, "ab")
            step(V.tensor_copy(ab[:, 0:2, :], p3(o, 3, 8)[:, 0:2, :]))
            free(V.tensor_copy(ab[0:64, 2, :], o[0:64, 16:24]), "ab")
            dve.wait_ge(s_misc, 64)
            step(TTo(u_dt[:, :, :], ab[:, :, 0:4], mid(hb[:, 0:4], 3), ALU.add))
            step(STT(out=absu[:, :, :], in0=u_dt[:, :, :], scalar=-1.0, in1=u_dt[:, :, :], op0=ALU.mult, op1=ALU.max),
                 ab_mid)
            dve.wait_ge(ab_exp, 1)
            step(STT(out=soft[:, :, :], in0=u_dt[:, :, :], scalar=0.0, in1=soft[:, :, :], op0=ALU.max, op1=ALU.add))
            step(STT(out=g_tm[:, :, :], in0=soft[:, :, :], scalar=-1.0, in1=mid(hb[:, 4:8], 3), op0=ALU.mult,
                     op1=ALU.mult))
            step(TS(beta[:, :, :], beta[:, :, :], 1.0, None, ALU.add))
            step(V.reciprocal(beta[:, :, :], beta[:, :, :]), g_ready)
            for t in range(8):
                dve.wait_ge(nrm_ready, t + 1)
                r = (oA if t < 4 else oB)[:, t % 4, :]
                step(STT(out=qkv[:, t, :], in0=qkv[:, t, :], scalar=DK_A ** -0.5 if t < 4 else 1.0, in1=r, op0=ALU.mult,
                         op1=ALU.mult), qk_ready)
            o = full(dve, "gc")
            for s in range(3):
                n = TILE_N[s]
                step(TS(gneg[0:n, s, :], o[0:n, 8 * s:8 * s + 4], -1.0, None, ALU.mult))
                step(TTo(kdf[0:n, s, :], o[0:n, 8 * s + 4:8 * s + 8], gneg[0:n, s, :], ALU.add))
            free(V.tensor_copy(glp[:, :, :], o[:, 0:16].rearrange("p (s z h) -> p s z h", s=2, z=2)[:, :, 1, :]), "gc")
            for h in range(HEADS):
                freed(dve, f"gB{h}")
                step(V.tensor_copy(glb[:, h, :], kbqg[:, 0, h, PROMPT:TOK].rearrange("p (b w) -> p b w", w=8)[:, :, 7]))
                step(TTo(kbqg[:, 1, h, :], kbqg[:, 0, h, :], qkv[:, h, :], ALU.mult))
                o = full(dve, f"bB{h}")
                step(TTo(qkv[:, 8 + h, :], o[:, 0:TOK], qkv[:, 8 + h, :], ALU.mult))
                free(TTo(oA[:, h, :], o[:, 0:TOK], qkv[:, 4 + h, :], ALU.mult), f"bB{h}")
                step(TTo(kbqg[:, 0, h, :], kbqg[:, 0, h, :], oA[:, h, :], ALU.mult), kb_ready)
            for s in range(3):
                n = TILE_N[s]
                m = triu if s < 2 else tri8
                step(STT(out=attnT[0:n, s, :, 0:n], in0=attnT[0:n, s, :, 0:n], scalar=1.0, in1=mid(m[0:n, 0:n], HEADS),
                         op0=ALU.min, op1=ALU.mult))
            dve.wait_ge(kdf_ready, 1)
            dve.wait_ge(out_sem, 32)
            for s in range(3):
                n = TILE_N[s]
                o = p3(full(dve, f"kT{s}"), HEADS, 128)
                free(TTo(kdT[0:n, s, :, :], o[0:n, :, :], last(kdf[0:n, s, :], 128), ALU.mult), f"kT{s}")
            for s in range(3):
                n = TILE_N[s]
                o = p3(full(dve, f"A{s}"), HEADS, 128)
                free(TTo(AT[0:n, s, :, 0:n], o[0:n, :, 0:n], attnT[0:n, s, :, 0:n], ALU.mult), f"A{s}")
                o = p3(full(dve, f"Q{s}"), HEADS, 128)
                free(TTo(attnT[0:n, s, :, 0:n], o[0:n, :, 0:n], attnT[0:n, s, :, 0:n], ALU.mult), f"Q{s}")

            def level(s, i, signal=None):
                n = TILE_N[s]
                step(TTo(LT[0:n, s, :, 0:n], AT[0:n, s, :, 0:n], mid(lvm[i][0:n, 0:n], HEADS), ALU.mult), signal)

            dve.wait_ge(silu_done, QT)
            full(dve, "tail2")
            for s in range(3):
                n = TILE_N[s]
                level(s, 0)
                step(TTo(TT[0:n, s, :, 0:n], mid(ident[0:n, 0:n], HEADS), LT[0:n, s, :, 0:n], ALU.subtract), t2t_ready)
            for s in range(3):
                level(s, 1, lt_ready)
            for i, b in enumerate(LEVELS):
                for s in range(3):
                    if i == 0 or b not in levels_of(s):
                        continue
                    n = TILE_N[s]
                    final = b == levels_of(s)[-1]
                    full(dve, f"X{s}{b}")
                    if not final:
                        level(s, i + 1, lt_ready)
                        o = p3(full(dve, f"Y{s}{b}"), HEADS, 128)
                        free(TTo(T_[0:n, s, :, 0:n], T_[0:n, s, :, 0:n], o[0:n, :, 0:n], ALU.subtract), f"Y{s}{b}")
                    o = p3(full(dve, f"Z{s}{b}"), HEADS, 128)
                    free(TTo(TT[0:n, s, :, 0:n], TT[0:n, s, :, 0:n], o[0:n, :, 0:n], ALU.subtract), f"Z{s}{b}")
            o = p3(full(dve, "ks1"), HEADS, 128)
            free(TTo(LT[:, 1, :, :], qkv[:, 8:12, 128:256], o[:, :, :], ALU.subtract), "ks1")
            o = p3(full(dve, "s1"), HEADS, 128)
            step(TTo(Sp[:, :, :], Sp[:, :, :], last(glp[:, 1, :], 128), ALU.mult))
            free(TTo(Sp[:, :, :], Sp[:, :, :], o[:, :, :], ALU.add), "s1")
            o = full(dve, "ks2")[:, :].rearrange("p (h z t) -> p h z t", h=HEADS, z=2)
            step(V.tensor_copy(oA[:, :, PROMPT:TOK], o[:, :, 1, :]), st_ready)
            free(TTo(LT[:, 2, :, 0:64], qkv[:, 8:12, PROMPT:TOK], o[:, :, 0, :], ALU.subtract), "ks2")
            o = p3(full(dve, "o2"), HEADS, 128)
            free(TTo(oA[:, :, PROMPT:TOK], oA[:, :, PROMPT:TOK], o[:, :, 0:64], ALU.add), "o2")
            Sg4 = Sg[:, :, :].rearrange("p (b h) e -> p b h e", h=HEADS)
            for h in range(HEADS):
                if h:
                    full(dve, f"ss{h - 1}1")
                step(TTo(VM[0:64, :, :], mid(R[0:64, 2, h, :], BATCHES), last(bsel[0:64, :], 128), ALU.mult), vm_ready)
                for f in range(2):
                    st = Sg4[:, 4 * f:4 * f + 4, h, :]
                    step(TTo(st, st, last(glb[:, h, 4 * f:4 * f + 4], 128), ALU.mult))
                    o = p3(full(dve, f"ss{h}{f}"), 4, 128)
                    free(TTo(st, st, o, ALU.add), f"ss{h}{f}")
            for h in range(HEADS):
                dve.wait_ge(onr_ready, h + 1)
                step(TTo(oA[:, h, :], oA[:, h, :], oB[:, h, :], ALU.mult))
                step(STT(out=oA[:, h, :], in0=oA[:, h, :], scalar=cols[:, 56:57], in1=zg[:, h, :], op0=ALU.mult,
                         op1=ALU.mult), o_ready if h == HEADS - 1 else None)

            step(V.memset(vTM[64:128, 2, :], 0.0))
            step(V.memset(AT[64:128, 2, :, :], 0.0))
            dve.wait_ge(la_act, 1)
            step(STT(out=eq[:, :, :], in0=G3[:, :, :], scalar=0.0, in1=ek[:, :, :], op0=ALU.min, op1=ALU.subtract))
            for t in range(2):
                step(V.tensor_tensor_scan(G3[:, t, :], rst[:, :], eq[:, t, :], 0.0, ALU.mult, ALU.add))
            step(TS(G3[:, :, :], G3[:, :, :], 1.0 / GATE_NORM, None, ALU.mult))

            def blocks(t, a, w, b):
                return t[:, :, a:a + w].rearrange("p f (n b) -> p f n b", b=b)

            def differences(parts, signal):
                for i, (a, w, b, r) in enumerate(parts):
                    g = blocks(G3, a, w, b)
                    ref = g[:, :, :, r:r + 1].to_broadcast([128, 2, w // b, b])
                    if signal:
                        step(TTo(blocks(eq, a, w, b), g, ref, ALU.subtract))
                    step(TTo(blocks(ek, a, w, b), ref, g, ALU.subtract), lev_sub if i == len(parts) - 1 else None)

            def attention(lv):
                for s in range(3 if lv == 0 else 2):
                    n = TILE_N[s]
                    m = (tri16 if s < 2 else tri8) if lv == 0 else lvm[lv + 3]
                    for r in range(2):
                        o = p3(full(dve, f"L{lv}{s}{r}"), 2, 128)
                        dst = AT[0:n, s, :, :].rearrange("p (a r) c -> p r a c", r=2)[:, r, :, 0:n]
                        if lv == 0:
                            free(TTo(dst, o[0:n, :, 0:n], mid(m[0:n, 0:n], 2), ALU.mult), f"L{lv}{s}{r}")
                        else:
                            free(TTo(Lp[0:n, 0:2, 0:n], o[0:n, :, 0:n], mid(m[0:n, 0:n], 2), ALU.mult), f"L{lv}{s}{r}")
                            step(TTo(dst, dst, Lp[0:n, 0:2, 0:n], ALU.add), at_ready if lv == 3 and r == 1 else None)

            for lv in range(4):
                w = TOK if lv == 0 else PROMPT
                b = 8 << lv
                differences([(0, PROMPT, 16, 0), (PROMPT, TOK - PROMPT, 8, 0)] if lv == 0 else
                            [(0, PROMPT, 2 * b, b - 1)], True)
                dve.wait_ge(lev_exp, lv + 1)
                if lv >= 2:
                    full(dve, f"L{lv - 2}{1 if lv > 2 else 2}1")
                step(STT(out=qt[:, lv % 2, :, 0:w], in0=eq[:, :, 0:w], scalar=1.0, in1=qb3[:, :, 0:w], op0=ALU.min,
                         op1=ALU.mult))
                if lv == 0:
                    step(TTo(kt[:, 0, :, :], ek[:, :, :], kb3[:, :, :], ALU.mult), lev_ready)
                else:
                    step(STT(out=kt[:, lv % 2, :, 0:w], in0=ek[:, :, 0:w], scalar=1.0, in1=kb3[:, :, 0:w], op0=ALU.min,
                             op1=ALU.mult), lev_ready)
                attention(lv)
            differences([(0, PROMPT, 128, 127), (PROMPT, TOK - PROMPT, 8, 7)], False)
            dve.wait_ge(lev_exp, 5)
            step(V.tensor_copy(gll[:, :, 0:2], blocks(eq, 0, PROMPT, 128)[:, :, :, 127]))
            step(V.tensor_copy(gll[:, :, 2:10], blocks(eq, PROMPT, TOK - PROMPT, 8)[:, :, :, 7]))
            step(TTo(qG[:, :, :], eq[:, :, :], qb3[:, :, :], ALU.mult))
            step(TTo(kdF[:, :, :], ek[:, :, :], kb3[:, :, :], ALU.mult), kd_ready)
            o = p3(full(dve, "gs1"), 2, 256)
            step(TTo(Slp[:, :, :], Slp[:, :, :], last(gll[:, :, 1], 128), ALU.mult))
            step(TTo(Slp[0:64, :, :], Slp[0:64, :, :], o[0:64, :, 0:128], ALU.add))
            free(TTo(Slp[64:128, :, :], Slp[64:128, :, :], o[64:128, :, 128:256], ALU.add), "gs1")
            Sl4 = Sl[:, :, :].rearrange("p (b a) e -> p b a e", a=2)
            for h in range(HEADS):
                r, hp = 64 * (h % 2), h // 2
                if h:
                    full(dve, f"gss{h - 1}1")
                else:
                    full(dve, "ob21")
                v = vTM[0:64, 2, 128 * h:128 * h + 128]
                step(TTo(VM[0:64, :, :], mid(v, BATCHES), last(bsel[0:64, :], 128), ALU.mult), vm_ready)
                for f in range(2):
                    st = Sl4[r:r + 64, 4 * f:4 * f + 4, hp, :]
                    step(TTo(st, st, last(gll[r:r + 64, hp, 2 + 4 * f:6 + 4 * f], 128), ALU.mult),
                         st_ready if h == 0 and f == 0 else None)
                    o = p3(full(dve, f"gss{h}{f}"), 4, 128)
                    free(TTo(st, st, o[r:r + 64, :, :], ALU.add), f"gss{h}{f}")
            for h in range(HEADS):
                dve.wait_ge(onr_ready, HEADS + h + 1)
                step(TTo(oB[:, h, :], oB[:, h, :], osq[:, h, :], ALU.mult))
                step(STT(out=oB[:, h, :], in0=oB[:, h, :], scalar=cols[:, 57:58], in1=zg[:, 4 + h, :], op0=ALU.mult,
                         op1=ALU.mult), o_ready if h == HEADS - 1 else None)

            for m in range(KD):
                freed(dve, f"ga{m}")
                freed(dve, f"gb{m}")
                o = full(dve, f"ua{m}")
                free(TTo(qb3[:, m % 2, :], o[:, 0:TOK], qb3[:, m % 2, :], ALU.mult), f"ua{m}")
                o = full(dve, f"ub{m}")
                free(TTo(kb3[:, m % 2, :], o[:, 0:TOK], kb3[:, m % 2, :], ALU.mult), f"ub{m}")
                step(TTo(merged[:, m, :], qb3[:, m % 2, :], kb3[:, m % 2, :], ALU.add), mrg_ready)
            dve.wait_ge(s_x2, 32)

            def add_rows(name, s, f):
                n = TILE_N[s]
                o = full(dve, name)
                v = x_tm[0:n, s, 512 * f:512 * f + 512]
                free(TTo(v, v, o[0:n, :], ALU.add), name)

            for s in range(3):
                for f in range(2):
                    add_rows(f"wo{s}{f}", s, f)
            dve.wait_ge(s_late, 64)
            for s in range(3):
                n = TILE_N[s]
                dve.wait_ge(x2_rs, s + 1)
                step(STT(out=h2[0:n, s, :], in0=x_tm[0:n, s, :], scalar=rs[0:n, 3 + s:4 + s], in1=n2b[0:n, :],
                         op0=ALU.mult, op1=ALU.mult), h2_ready)
            step(V.memset(gate_all[:, :, :], 0.0))
            step(V.memset(slot_all[:, :, :], -1.0))
            for s in range(3):
                n = TILE_N[s]
                o = full(dve, f"lg{s}")
                free(TTo(lgt[0:n, s, :], o[0:n, 0:EXPERTS], brt[0:n, :], ALU.add), f"lg{s}")
                step(V.max(rt8[0:n, s, :], lgt[0:n, s, :]))
                step(V.max_index(ri8[0:n, s, :], rt8[0:n, s, :], lgt[0:n, s, :]))
                step(V.tensor_copy(rif[0:n, s, :], ri8[0:n, s, :]))
                step(TS(rneg[0:n, s, 0:1], rt8[0:n, s, 0:1], -1.0, None, ALU.mult), route_max)
            for s in range(3):
                n = TILE_N[s]
                dve.wait_ge(route_exp, s + 1)
                step(V.reciprocal(rneg[0:n, s, 1:2], rneg[0:n, s, 1:2]))
                step(TS(rg4[0:n, s, :], rg4[0:n, s, :], rneg[0:n, s, 1:2], None, ALU.mult))
                gate = gate_all[0:n, s, 0:EXPERTS]
                for k in range(TOP):
                    dst = gate if k == 0 else tmp32[0:n, :]
                    step(TS(dst, iota[0:n, 0:EXPERTS], rif[0:n, s, k:k + 1], rg4[0:n, s, k:k + 1], ALU.is_equal, ALU.mult))
                    if k:
                        step(TTo(gate, gate, tmp32[0:n, :], ALU.add))
                step(TS(msk[0:n, s, :], gate, 0.0, None, ALU.is_gt), gate_ready if s == 2 else None)
                more = gate_all[0:n, s, EXPERTS:EXPERTS * ROUNDS].rearrange("p (r e) -> p r e", e=EXPERTS)
                step(V.tensor_copy(more, mid(gate, ROUNDS - 1)))
            for s in range(3):
                n = TILE_N[s]
                o = full(dve, f"sl{s}")
                free(TTo(tmp32[0:n, :], o[0:n, 0:EXPERTS], msk[0:n, s, :], ALU.mult), f"sl{s}")
                for r in range(ROUNDS):
                    step(TS(slot_all[0:n, s, EXPERTS * r:EXPERTS * r + EXPERTS], tmp32[0:n, :], -1.0 - SLOTS * r, None,
                            ALU.add))
            o = full(dve, "cnt")
            free(V.reduce_max(cmax[:, 0:1], o[:, 0:EXPERTS], AX_X), "cnt")
            step(TS(cmax[:, 1:1 + ROUNDS], iota[:, 0:ROUNDS], float(SLOTS), cmax[:, 0:1], ALU.mult, ALU.is_lt))
            step(V.reduce_sum(cmax[:, 6:7], cmax[:, 1:1 + ROUNDS], AX_X))
            step(TS(nit[:, 0:1], cmax[:, 6:7], float(PAIRS), None, ALU.mult))
            step(TS(nit[:, 1:2], cmax[:, 6:7], float(EXPERTS), None, ALU.mult), cnt_ready)
            for s in range(3):
                for f in range(2):
                    add_rows(f"bd{s}{f}", s, f)

            def link(ins, s, value):
                ins.then_inc(s, 1)
                dve.wait_ge(s, value)

            def one_hot(dst, x, col):
                c = slot_all[:, :, bass.ds(col, 1)].to_broadcast([128, 3, SLOTS])
                return TTo(dst[:, :, SLOTS * x:SLOTS * x + SLOTS], mid(iota[:, :], 3), c, ALU.is_equal)

            step(V.memset(y_sl[:, :], 0.0), yt_done)
            step(V.memset(GTs[:, :], 0.0), gtr_done)
            step(one_hot(Psel, 0, 0))
            step(one_hot(Psel, 1, 1), p_ready)
            its = dve.value_load(nit[0:1, 0:1], min_val=PAIRS, max_val=PAIRS * ROUNDS)
            CH = 12

            def scattered(n, j0):
                for j in range(j0, j0 + 3):
                    s, f = j // 2, j % 2
                    rows_n = TILE_N[s]
                    if j % 2:
                        dve.wait_ge(m_full[6], b6(n, j // 2))
                    else:
                        dve.wait_ge(m_full[7], b7(n, j // 2))
                    v = x_tm[0:rows_n, s, 512 * f:512 * f + 512]
                    link(TTo(v, v, bank[7 - j % 2][0:rows_n, :], ALU.add), acc_done, n * 6 + (j + 1))

            with dve.Fori(0, its) as n:
                k = [0]

                def inner(ins):
                    k[0] += 1
                    link(ins, m_dve, n * CH + k[0])

                dve.wait_ge(m_full[6], n * 4 + 1)
                inner(one_hot(Psel, 0, n * 2 + 2))
                link(one_hot(Psel, 1, n * 2 + 3), p_ready, n + 2)
                dve.wait_ge(m_full[7], n * 5 + 1)
                for y in range(2):
                    inner(one_hot(Gsel, y, n * 2 + y))
                    g = gate_all[:, :, bass.ds(n * 2 + y, 1)].to_broadcast([128, 3, SLOTS])
                    part = Gsel[:, :, SLOTS * y:SLOTS * y + SLOTS]
                    if y == 0:
                        inner(TTo(part, part, g, ALU.mult))
                    else:
                        link(TTo(part, part, g, ALU.mult), gm_ready, n + 1)
                scattered(n, 0)
                for x in range(2):
                    dve.wait_ge(t_full, n * 2 + (x + 1))
                    e = n % PAIRS
                    for dst, b, c0 in ((gbuf, FMB[0], 0), (ubuf, FMB[1], FT)):
                        bias = bcol[:, bass.ds(e * 32 + (16 * x + c0), FT)].rearrange("p (h j) -> p j h", h=2)
                        bias = bias.unsqueeze(3).to_broadcast([128, 4, 2, SLOTS])
                        src = bank[b][:, :].rearrange("p (j h t) -> p j h t", j=4, h=2)
                        inner(TTo(dst[:, :, :, :], src, bias, ALU.add))
                        if c0 == 0:
                            link(TS(gbuf[:, :, :, :], gbuf[:, :, :, :], LIMIT, None, ALU.min), pre_sig, n * 2 + (x + 1))
                    inner(TS(ubuf[:, :, :, :], ubuf[:, :, :, :], LIMIT, -LIMIT, ALU.min, ALU.max))
                    inner(STT(out=ubuf[:, :, :, :], in0=ubuf[:, :, :, :], scalar=1.0, in1=gbuf[:, :, :, :], op0=ALU.add,
                              op1=ALU.mult))
                    dve.wait_ge(sg_ready, n * 2 + (x + 1))
                    link(TTo(hm[x], ubuf[:, :, :, :], sbuf_[:, :, :, :], ALU.mult), hm_ready, n * 2 + (x + 1))
                    if x == 0:
                        scattered(n, 3)
                assert k[0] == CH, k
            scattered(its, 0)
            scattered(its, 3)
            for s in range(3):
                n = TILE_N[s]
                dve.wait_ge(fin_act, s + 1)
                step(STT(out=x_tm[0:n, s, :], in0=x_tm[0:n, s, :], scalar=rs[0:n, s:s + 1], in1=nfb[0:n, :],
                         op0=ALU.mult, op1=ALU.mult), fin_dve)


_INS = ["x_prompt", "x_sample", "state_gdn", "state_gdn_conv", "state_gla", "norm1_w", "w_in", "conv_w", "a_log",
        "dt_bias", "gdn_norm_w", "gla_gk_up", "gla_gk_b", "gla_norm_w", "w_up_a", "w_up_b", "w_o", "norm2_w",
        "w_router", "b_router", "w_gate_up", "b_gate_up", "w_down", "b_down", "norm_f_w"]
_OUTS = [(1, PROMPT, D), (BATCHES, STEPS, D), (1, 1, HEADS, DK_A, DV), (1, 1, 3, QKV), (1, 1, HEADS, DK_B, DV),
         (1, BATCHES, HEADS, DK_A, DV), (1, BATCHES, 3, QKV), (1, BATCHES, HEADS, DK_B, DV)]


def kernel(**inputs):
    import numpy as _np
    import concourse.bacc as _bacc
    from concourse import mybir as _mybir
    from concourse.bass_utils import run_bass_kernel_spmd as _run

    nc = _bacc.Bacc("TRN2", target_bir_lowering=False, num_devices=1)
    arrays, args = {}, []
    for name in _INS:
        a = _np.ascontiguousarray(inputs[name])
        arrays[f"in_{name}_dram"] = a
        args.append(nc.dram_tensor(f"in_{name}_dram", a.shape, _mybir.dt.from_np(a.dtype), kind="ExternalInput").ap())
    for i, shape in enumerate(_OUTS):
        args.append(nc.dram_tensor(f"out_{i}_dram", shape, F32, kind="ExternalOutput").ap())
    build(nc, *args)
    r = _run(nc, [arrays], core_ids=[0])
    return tuple(r.results[0][f"out_{i}_dram"] for i in range(len(_OUTS)))
```

```python
from contextlib import ExitStack

import concourse.bass as bass
from concourse import mybir

F32 = mybir.dt.float32
U32 = mybir.dt.uint32
I32 = mybir.dt.int32
ALU = mybir.AluOpType
ACT = mybir.ActivationFunctionType
AX_X = mybir.AxisListType.X

D = 1024
KD = D // 128
HEADS = 4
DK_A, DV = 128, 128
DK_B = 64
QKV = 3 * HEADS * 128
QT = QKV // 128
PROMPT, BATCHES, STEPS = 256, 8, 8
TOK = PROMPT + BATCHES * STEPS
TILE_N = [128, 128, 64]
TILE_0 = [0, 128, 256]
RANK = 16
EXPERTS, TOP, FF = 32, 4, 1024
FT = FF // 128
EPS = 1e-6
GATE_NORM = 16.0
LIMIT, ALPHA = 7.0, 1.702
SLOTS = 64
ROUNDS = TOK // SLOTS
PAIRS = EXPERTS // 2
CATN = 3 + PROMPT + BATCHES * (3 + STEPS)
CATS = 3 + PROMPT
CONVN = CATN - 3

C_QKV, C_Z, C_AB = 0, 1536, 2048
C_QB, C_KB, C_VB, C_GB, C_LR, C_GA, C_GBB = 2056, 2312, 2568, 3080, 3592, 3608, 4632

RING = 12
MIX = 5
MIX_PANELS = 26
WO = 4
RING_USES = [-(-(MIX_PANELS - c) // MIX) if c < MIX else (1 if c < MIX + WO else 0) for c in range(RING)]

LEVELS = [1, 2, 4, 8, 16, 32, 64]


def levels_of(s):
    return LEVELS if s < 2 else LEVELS[:3]


def psum_order():
    o = ["cols", "cst"]
    o += [f"xT{s}{f}" for s in range(3) for f in range(2)]
    o += [f"qkv{t}" for t in range(QT)]
    o += ["ab"] + [f"nrm{t}" for t in range(4)] + ["lr", "qb0", "qb1", "gk0", "gk1"]
    o += [f"nrm{t}" for t in range(4, 8)] + ["kb0", "kb1", "z0", "z1", "z2"]
    fill = [["gc", "z3"], ["vb0"] + [f"tail{g}" for g in range(3)], ["vb1"], ["vb2"]]
    for lv in range(4):
        o += [f"L{lv}{s}{r}" for s in range(3 if lv == 0 else 2) for r in range(2)] + fill[lv]
    o += [f"gT{s}" for s in range(3)]
    for h in range(HEADS):
        o += [f"gB{h}", f"bB{h}", f"g{h}"]
        if h < 3:
            o += [f"ob{h}0", f"ob{h}1"] + ([f"gs{h}"] if h < 2 else [])
    o += [f"kT{s}" for s in range(3)] + [f"om{h}" for h in range(HEADS)]
    for s in range(3):
        o += [f"A{s}", f"Q{s}"]
    o += [f"t2{s}" for s in range(3)]
    for b in LEVELS[1:]:
        for s in range(3):
            if b in levels_of(s):
                o += [f"X{s}{b}"]
        for s in range(3):
            if b in levels_of(s):
                o += ([f"Y{s}{b}"] if b != levels_of(s)[-1] else []) + [f"Z{s}{b}"]
    o += ["rt0", "ga0", "v0", "gb0", "o0", "s0", "ga1", "ks1", "gb1", "rt1", "ga2", "v1", "gb2", "o1", "s1", "ks2",
          "rt2", "v2", "o2", "ga3"] + [f"on{h}" for h in range(HEADS)] + ["gb3"]
    for m in range(KD):
        if m < HEADS:
            o += [f"ss{m}0", f"ss{m}1", f"gss{m}0", f"gss{m}1"]
        else:
            o += [f"ga{m}", f"gb{m}"]
        o += [f"ua{m}", f"ub{m}"]
    o += ["wo00", "wo01", "bgu", "wo10", "hT00", "hT01", "wo11", "lg0", "wo2", "hT10", "hT11", "lg1"]
    o += ["hT20", "hT21", "lg2"] + [f"sl{s}" for s in range(3)] + ["cnt", "wT"]
    return o


PSUM_USE = {name: (i % 8, i // 8) for i, name in enumerate(psum_order())}


def build(nc, x_prompt, x_sample, state_gdn, state_gdn_conv, state_gla, norm1_w, w_in, conv_w, a_log, dt_bias,
          gdn_norm_w, gla_gk_up, gla_gk_b, gla_norm_w, w_up_a, w_up_b, w_o, norm2_w, w_router, b_router,
          w_gate_up, b_gate_up, w_down, b_down, norm_f_w, y_prompt, y_sample, gdn_p, conv_p, gla_p, gdn_s,
          conv_s, gla_s):
    with ExitStack() as ctx:
        def sb(name, shape, dt=F32):
            return ctx.enter_context(nc.sbuf_tensor(name, shape, dt))

        def sem(name):
            return ctx.enter_context(nc.semaphore(name))

        def flat(t, a, shape):
            n = 1
            for k in shape:
                n *= k
            v = t[:, a:a + n]
            if len(shape) == 1:
                return v
            names = "abcd"[:len(shape)]
            return v.rearrange("p (" + " ".join(names) + ") -> p " + " ".join(names),
                               **dict(zip(names[1:], shape[1:])))

        ring = sb("ring", [128, RING * 2048])

        def slot(i):
            return ring[:, i * 2048:(i + 1) * 2048]

        ATg = flat(ring, MIX * 2048, (3, HEADS, 128))
        W0 = (MIX + 1) * 2048
        AT = flat(ring, W0, (3, HEADS, 128))
        attnT = flat(ring, W0 + 1536, (3, HEADS, 128))
        kbqg = flat(ring, W0 + 3072, (2, HEADS, TOK))
        W1 = W0 + 3072 + 2560
        cat = flat(ring, W1, (QT, CATN))
        T_ = flat(ring, W1, (3, HEADS, 128))
        TT = flat(ring, W1 + 1536, (3, HEADS, 128))
        X1 = flat(ring, W1 + 3072, (3, HEADS, 128))
        LT = flat(ring, W1 + 4608, (3, HEADS, 128))
        assert W1 + 6144 + 512 <= RING * 2048
        eq = flat(ring, W1 + 4608, (2, TOK))
        ek = flat(ring, W1 + 5248, (2, TOK))
        qt = flat(ring, W0 + 3072, (2, 2, TOK))
        kt = flat(ring, W0 + 4352, (2, 2, TOK))
        osq = flat(ring, W1 + 1280, (HEADS, TOK))
        VM = [flat(ring, W0 + 3072 + 1024 * i, (BATCHES, 128)) for i in range(2)]

        xbuf = sb("xbuf", [128, 3 * D])
        x_tm = flat(xbuf, 0, (3, D))
        R = flat(xbuf, 0, (3, HEADS, 128))
        gsq = flat(xbuf, 0, (HEADS, TOK))
        kdT = flat(xbuf, 1536, (3, HEADS, 128))
        tail_tm = flat(xbuf, 1536, (QKV,))
        hTb = sb("hTb", [128, KD * TOK])
        hT = flat(hTb, 0, (KD, TOK))
        h2b = sb("h2b", [128, QT * TOK])
        qkv = flat(h2b, 0, (QT, TOK))
        merged = flat(ring, (MIX + WO) * 2048, (KD, TOK))
        gate_b23 = flat(ring, W1 + 3072, (2, TOK))
        zgb = sb("zgb", [128, 8 * TOK])
        zg = flat(zgb, 0, (8, TOK))
        cst_rows = zgb[0:24, 0:QKV]
        qb = sb("qb", [128, 2 * TOK])
        kb = sb("kb", [128, 2 * TOK])
        Gc = sb("Gc", [128, 2 * TOK])
        qb3, kb3, G3 = (flat(t, 0, (2, TOK)) for t in (qb, kb, Gc))
        vTM = sb("vTM", [128, 3, 512])
        oAb = sb("oAb", [128, HEADS * TOK])
        oBb = sb("oBb", [128, HEADS * TOK])
        oA = flat(oAb, 0, (HEADS, TOK))
        oB = flat(oBb, 0, (HEADS, TOK))
        Sg = sb("Sg", [128, BATCHES * HEADS, 128])
        bcol = Sg[:, 12:16, :].rearrange("p a b -> p (a b)")
        Sl = sb("Sl", [128, BATCHES * 2, 128])
        Sp = sb("Sp", [128, HEADS, 128])
        Slp = sb("Slp", [128, 2, 128])
        cv = sb("cv", [128, 2, CATN])
        kdG = [flat(cv[:, :, :].rearrange("p a b -> p (a b)"), 256 * i, (2, 128)) for i in range(2)]
        kdG.append(flat(ring, MIX * 2048 + 1536, (2, 128)))
        kdG = [t.rearrange("p a b -> p (a b)") for t in kdG]
        gate_a = [qb3[:, 0, :], qb3[:, 1, :], G3[:, 0, :], G3[:, 1, :]]
        gate_b = [kb3[:, 0, :], kb3[:, 1, :], gate_b23[:, 0, :], gate_b23[:, 1, :]]
        tails = flat(ring, W0 + 768, (QT, 27))
        rows = sb("rows", [64, 128])
        cols = sb("cols", [128, 64])
        Lp = flat(ring, W0 + 1152, (2, 128))
        w_small = flat(ring, W0, (KD, 24))
        gk_up = ring[0:RANK, W0 + 192:W0 + 448]
        lrT = ring[0:RANK, W0 + 448:W0 + 768]
        lr_tm = flat(ring, W0 + 1092, (3, RANK))
        ab = sb("ab", [128, 3, 8])
        hb = sb("hb", [128, 8])
        u_dt = sb("u_dt", [128, 3, HEADS])
        absu = sb("absu", [128, 3, HEADS])
        soft = sb("soft", [128, 3, HEADS])
        beta = sb("beta", [128, 3, HEADS])
        g_tm = sb("g_tm", [128, 3, HEADS])
        kdf = sb("kdf", [128, 3, HEADS])
        glp = sb("glp", [128, 2, HEADS])
        glb = sb("glb", [128, HEADS, BATCHES])
        gll = sb("gll", [128, 2, 10])
        gneg = sb("gneg", [128, 3, HEADS])
        ss = sb("ss", [128, 8])
        rs = sb("rs", [128, 8])
        rt8 = sb("rt8", [128, 3, 8])
        ri8 = sb("ri8", [128, 3, 8], U32)
        rif = sb("rif", [128, 3, 8])
        rg4 = sb("rg4", [128, 3, 4])
        rneg = sb("rneg", [128, 3, 2])
        lgt = sb("lgt", [128, 3, EXPERTS])
        msk = sb("msk", [128, 3, EXPERTS])
        slot1 = sb("slot1", [128, 3, EXPERTS])
        cmax = sb("cmax", [128, 8])
        nit = sb("nit", [128, 2], I32)
        wr = sb("wr", [128, KD, EXPERTS])
        brt = sb("brt", [128, EXPERTS])

        ident = sb("ident", [128, 128])
        ones = sb("ones", [128, 128])
        triu = sb("triu", [128, 128])
        blk = flat(ring, W0 + 1536, (6, 128))
        lvm_hi = sb("lvm_hi", [128, 3, 128])
        lvm_lo = flat(ring, W1 + 6144, (4, 128))
        lvm = [lvm_lo[:, i, :] for i in range(4)] + [lvm_hi[:, i, :] for i in range(3)]
        tri8 = sb("tri8", [128, 128])
        tri16 = sb("tri16", [128, 128])
        b8 = sb("b8", [64, 64])
        bsel = sb("bsel", [128, BATCHES])
        rst = sb("rst", [128, TOK])
        eps = sb("eps", [128, 1])
        iota = sb("iota", [128, SLOTS])

        bank = [ctx.enter_context(nc.psum_tensor(f"bank{i}", [128, 512], F32)) for i in range(8)]

        xTe = flat(zgb, 0, (KD, 2 * SLOTS))
        pre = flat(zgb, 1024, (2, 512))
        y_sl = flat(hTb, 0, (D,))
        Psel = flat(hTb, 1024, (3, 2 * SLOTS))
        Gsel = flat(hTb, 1408, (3, 2 * SLOTS))
        GTs = flat(hTb, 1792, (TOK,))
        hm = [flat(zgb, 2048, (4, 2, SLOTS)), flat(cv[:, :, :].rearrange("p a b -> p (a b)"), 0, (4, 2, SLOTS))]
        gbuf = flat(qb, 0, (4, 2, SLOTS))
        ubuf = flat(kb, 0, (4, 2, SLOTS))
        sbuf_ = flat(Gc, 0, (4, 2, SLOTS))
        NCOL = ROUNDS * EXPERTS + 2
        vflat = vTM[:, :, :].rearrange("p a b -> p (a b)")
        slot_all = flat(vflat, 0, (3, NCOL))
        gate_all = flat(vflat, 3 * NCOL, (3, NCOL))
        h2 = flat(h2b, 0, (3, D))
        bdn = Sg[0:EXPERTS, 0:8, :].rearrange("e a b -> e (a b)")
        n2b, nfb = oAb[:, 0:D], oBb[:, 0:D]
        PRE, FMB, DN = (0, 1), (2, 3), (4, 5)

        wo_half = zgb[0:64, 1024:1536]

        wfull = [sem(f"wfull{i}") for i in range(RING)]
        wfree = [sem(f"wfree{i}") for i in range(RING)]
        pfull = [sem(f"pfull{i}") for i in range(8)]
        pfree = [sem(f"pfree{i}") for i in range(8)]
        s_x = [sem(f"x_in{i}") for i in range(3)]
        s_rows, s_small, s_misc, s_state = (sem(n) for n in (
            "rows_in", "small_in", "misc_in", "state_in"))
        s_x2, s_late = sem("x_again"), sem("late_in")
        consts = sem("consts")
        act_c, dve_c, pool_c = sem("act_chain"), sem("dve_chain"), sem("pool_chain")
        rs_ready, xs_ready = sem("rs_ready"), sem("xs_ready")
        conv_done, silu_done = sem("conv_done"), sem("silu_done")
        tails_ready = sem("tails_ready")
        sq_ready, nrm_ready, qk_ready = sem("sq_ready"), sem("nrm_ready"), sem("qk_ready")
        lr_ready = sem("lr_ready")
        ab_exp, ab_mid, g_ready = sem("ab_exp"), sem("ab_mid"), sem("g_ready")
        gneg_ready, dt_exp, kdf_ready, kb_ready = sem("gneg_ready"), sem("dt_exp"), sem("kdf_ready"), sem("kb_ready")
        dt_ready = sem("dt_ready")
        lt_ready, t2t_ready, inv_ready = sem("lt_ready"), sem("t2t_ready"), sem("inv_ready")
        rt_ready, vm_ready, st_ready = sem("rt_ready"), sem("vm_ready"), sem("st_ready")
        osq_ready, onr_ready, gn_ready, o_ready = sem("osq_ready"), sem("onr_ready"), sem("gn_ready"), sem("o_ready")
        la_act, la_ready, lev_sub, lev_exp, lev_ready = (sem(n) for n in (
            "la_act", "la_ready", "lev_sub", "lev_exp", "lev_ready"))
        at_ready, kd_ready, qg_ready = sem("at_ready"), sem("kd_ready"), sem("qg_ready")
        sig_ready, mrg_ready = sem("sig_ready"), sem("mrg_ready")
        x2_ready, x2_rs, h2_ready, half_ready, route_max, route_exp, mask_ready, gate_ready, slot_ready, cnt_ready = (sem(n) for n in (
            "x2_ready", "x2_rs", "h2_ready", "half_ready", "route_max", "route_exp", "mask_ready", "gate_ready", "slot_ready", "cnt_ready"))
        out_sem, y_out = sem("outputs"), sem("y_out")
        fin_act, fin_dve = sem("fin_act"), sem("fin_dve")
        m_full = {b: sem(f"mfull{b}") for b in (6, 7)}
        m_act, m_dve = sem("moe_act_chain"), sem("moe_dve_chain")
        xg_done, yt_done, t_full, gtr_done = sem("xg_done"), sem("yt_done"), sem("t_full"), sem("gtr_done")
        pre_done = sem("pre_done")
        acc_done, p_ready, gm_ready, hm_ready, sg_ready, pre_sig = (sem(n) for n in (
            "acc_done", "p_ready", "gm_ready", "hm_ready", "sg_ready", "pre_sig"))

        def mid(ap2, n):
            return ap2.unsqueeze(1).to_broadcast([ap2.shape[0], n, ap2.shape[1]])

        def last(ap2, n):
            return ap2.unsqueeze(2).to_broadcast([ap2.shape[0], ap2.shape[1], n])

        def full(eng, name):
            b, u = PSUM_USE[name]
            eng.wait_ge(pfull[b], u + 1)
            return bank[b]

        def freed(eng, name):
            b, u = PSUM_USE[name]
            eng.wait_ge(pfree[b], u + 1)

        def chain(eng, own):
            count = {}

            def step(ins, signal=None):
                s = signal or own
                count[s.name] = count.get(s.name, 0) + 1
                ins.then_inc(s, 1)
                eng.wait_ge(s, count[s.name])

            def free(ins, name):
                b, u = PSUM_USE[name]
                ins.then_inc(pfree[b], 1)
                eng.wait_ge(pfree[b], u + 1)
            return step, free

        def p3(bk, a, b):
            return bk[:, 0:a * b].rearrange("p (a b) -> p a b", b=b)

        def win(c0, n=256):
            return w_in[0][:, c0:c0 + n].rearrange("(k p) n -> p k n", p=128)

        panels = [win(C_QKV + 256 * i) for i in range(6)] + [win(C_QB), win(C_KB)]
        panels += [win(C_Z + 256 * i) for i in range(2)] + [win(C_VB), win(C_VB + 256), win(C_GB), win(C_GB + 256)]
        for f in range(2):
            ups = [w[0][:, 512 * f:512 * f + 512].rearrange("(k p) n -> p k n", p=128) for w in (w_up_a, w_up_b)]
            gates = [win(c + 512 * f + 256 * i) for i in range(2) for c in (C_GA, C_GBB)]
            panels += gates + ups if f == 0 else gates[:2] + ups + gates[2:]
        assert len(panels) == MIX_PANELS
        last_use = [f"qkv{2 * i + 1}" for i in range(6)] + ["qb1", "kb1", "z1", "z3", "vb2", "vb2", "g1", "g3"]
        for f in range(2):
            ups = [f"ua{4 * f + 3}", f"ub{4 * f + 3}"]
            gates = [f"{nm}{4 * f + 2 * i + 1}" for i in range(2) for nm in ("ga", "gb")]
            last_use += gates + ups if f == 0 else gates[:2] + ups + gates[2:]
        P_QB, P_KB, P_Z, P_VB, P_GB, P_M = 6, 7, 8, 10, 12, 14

        def expert_chunk(e, c):
            if c < 8:
                return w_gate_up[0][e, 128 * c:128 * c + 128, :] if isinstance(e, int) else \
                    w_gate_up[0][bass.ds(e, 1), 128 * c:128 * c + 128, :].rearrange("e p n -> p (e n)")
            r = 256 * (c - 8)
            if isinstance(e, int):
                return w_down[0][e, r:r + 256, :].rearrange("(k p) n -> p k n", p=128)
            return w_down[0][bass.ds(e, 1), r:r + 256, :].rearrange("e (k p) n -> p (e k) n", p=128)

        def chunk_dst(c):
            return slot(c) if c < 8 else slot(c).rearrange("p (k n) -> p k n", k=2)

        block = ctx.enter_context(nc.Block())

        @block.sync
        def _(sp):
            for s in range(2):
                sp.dma_start(x_tm[:, s, :], x_prompt[0, 128 * s:128 * s + 128, :]).then_inc(s_x[s], 16)
            sp.dma_start(x_tm[0:64, 2, :], x_sample.rearrange("b t d -> (b t) d")).then_inc(s_x[2], 16)
            sp.dma_start(rows[0:8, :], norm1_w[0].rearrange("(k p) -> k p", p=128)).then_inc(s_rows, 16)
            sp.dma_start(rows[8:56, :], conv_w[0].rearrange("j (t p) -> (j t) p", p=128)).then_inc(s_rows, 16)
            sp.dma_start(rows[56:57, :], gdn_norm_w).then_inc(s_rows, 16)
            sp.dma_start(rows[57:58, :], gla_norm_w).then_inc(s_rows, 16)
            sp.dma_start(rows[58:60, :], gla_gk_b[0].rearrange("(k p) -> k p", p=128)).then_inc(s_rows, 16)
            sp.dma_start(cst_rows, state_gdn_conv[0].rearrange("b w c -> (b w) c")).then_inc(s_rows, 16)
            for i in range(MIX):
                n = panels[i].shape[1]
                sp.dma_start(slot(i).rearrange("p (k n) -> p k n", k=n), panels[i]).then_inc(wfull[i], 16)
                if i == 0:
                    sp.dma_start(w_small[:, :, 0:8], win(C_AB, 8)).then_inc(s_small, 16)
                    sp.dma_start(w_small[:, :, 8:24], win(C_LR, 16)).then_inc(s_small, 16)
                    sp.dma_start(gk_up[:, :], gla_gk_up[0]).then_inc(s_small, 16)
                    sp.dma_start(hb[:, 0:4], dt_bias.to_broadcast([128, 4])).then_inc(s_misc, 16)
                    sp.dma_start(hb[:, 4:8], a_log.to_broadcast([128, 4])).then_inc(s_misc, 16)
            sp.dma_start(Sg[:, :, :], state_gdn[0].rearrange("b h d e -> d (b h) e")).then_inc(s_state, 16)
            sp.dma_start(Sl[:, :, :], state_gla[0].rearrange("b h d e -> (b h d) e")
                         .rearrange("(n p) e -> p n e", p=128)).then_inc(s_state, 16)
            sp.dma_start(wr[:, :, :], w_router[0].rearrange("(k p) e -> p k e", p=128)).then_inc(s_misc, 16)
            sp.dma_start(brt[:, :], b_router.to_broadcast([128, EXPERTS])).then_inc(s_misc, 16)
            for i in range(MIX, MIX_PANELS):
                full(sp, last_use[i - MIX])
                n = panels[i].shape[1]
                sp.dma_start(slot(i % MIX).rearrange("p (k n) -> p k n", k=n), panels[i]).then_inc(wfull[i % MIX], 16)
                if i == P_M + 8:
                    sp.wait_ge(o_ready, 2)
                    full(sp, f"gss{HEADS - 1}1")
                    for k in range(WO):
                        src = w_o[0][256 * k:256 * k + 256, :].rearrange("(k p) n -> p k n", p=128)
                        sp.dma_start(slot(MIX + k).rearrange("p (k n) -> p k n", k=2), src).then_inc(wfull[MIX + k], 16)
            c = RING - 1
            sp.dma_start(chunk_dst(c), expert_chunk(0, c)).then_inc(wfull[c], 16)
            for i in range(MIX_PANELS - MIX, MIX_PANELS):
                full(sp, last_use[i])
                c = i % MIX
                sp.dma_start(chunk_dst(c), expert_chunk(0, c)).then_inc(wfull[c], 16)
            full(sp, "wo2")
            for c in range(MIX, RING - 1):
                sp.dma_start(chunk_dst(c), expert_chunk(0, c)).then_inc(wfull[c], 16)

            def load_expert(e, e_mod):
                for c in range(RING):
                    sp.wait_ge(wfree[c], e)
                    sp.dma_start(chunk_dst(c), expert_chunk(e_mod, c)).then_inc(wfull[c], 16)

            with sp.Fori(1, EXPERTS) as e:
                load_expert(e, e)
            sp.wait_ge(cnt_ready, 1)
            its = sp.value_load(nit[0:1, 1:2], min_val=EXPERTS, max_val=EXPERTS * ROUNDS)
            with sp.If(its > EXPERTS):
                with sp.Fori(EXPERTS, its) as e:
                    load_expert(e, e % EXPERTS)
            for s in range(2):
                sp.wait_ge(fin_dve, s + 1)
                sp.dma_start(y_prompt[0, 128 * s:128 * s + 128, :], x_tm[:, s, :]).then_inc(y_out, 16)
            sp.wait_ge(fin_dve, 3)
            sp.dma_start(y_sample.rearrange("b t d -> (b t) d"), x_tm[0:64, 2, :]).then_inc(y_out, 16)
            sp.wait_ge(out_sem, 16 * 6)
            sp.wait_ge(y_out, 48)

        @block.gpsimd
        def _(pool):
            step, _ = chain(pool, pool_c)

            def select(out, in_, pattern, base, mult, op=ALU.is_ge, fill=0.0):
                step(pool.affine_select(out=out, in_=in_, pattern=pattern, base=base, channel_multiplier=mult,
                                        compare_op=op, fill=fill))

            step(pool.memset(eps[:, :], EPS), consts)
            step(pool.memset(ident[:, :], 0.0))
            select(ident[:, :], ident[:, :], [[-1, 128]], 0, 1, ALU.not_equal, 1.0)
            step(pool.memset(ones[:, :], 1.0), consts)
            select(triu[:, :], ones[:, :], [[1, 128]], 0, -1)
            for i, b in enumerate(LEVELS[1:]):
                v = blk[:, i, :].rearrange("p (n b) -> p n b", b=b)
                o = ones[:, :].rearrange("p (n b) -> p n b", b=b)
                select(v, o, [[-b, 128 // b], [0, b]], 0, 1)
                select(v, v, [[b, 128 // b], [0, b]], b - 1, -1)
            step(pool.tensor_tensor(tri8[:, :], triu[:, :], blk[:, 2, :], ALU.mult))
            step(pool.tensor_tensor(tri16[:, :], triu[:, :], blk[:, 3, :], ALU.mult))
            for i in range(7):
                big = blk[:, i, :] if i < 6 else ones[:, :]
                small = blk[:, i - 1, :] if i > 0 else ident[:, :]
                step(pool.tensor_tensor(lvm[i], big, small, ALU.subtract))
                step(pool.tensor_tensor(lvm[i], lvm[i], triu[:, :], ALU.mult))
            step(pool.tensor_copy(b8[:, :], blk[0:64, 2, 0:64]))
            step(pool.memset(bsel[:, :], 1.0))
            select(bsel[:, :], bsel[:, :], [[-8, 8]], 0, 1)
            select(bsel[:, :], bsel[:, :], [[8, 8]], 7, -1)
            step(pool.memset(rst[:, :], 1.0))
            step(pool.memset(rst[:, 0:256].rearrange("p (n b) -> p n b", b=128)[:, :, 0:1], 0.0))
            step(pool.memset(rst[:, 256:TOK].rearrange("p (n b) -> p n b", b=8)[:, :, 0:1], 0.0))
            step(pool.iota(iota[:, :], pattern=[[1, SLOTS]], base=0, channel_multiplier=0,
                           allow_small_or_imprecise_dtypes=True))
            step(pool.memset(ab[:, :, :], 0.0), consts)

            freed(pool, "tail2")
            pool.dma_start(conv_p[0, 0], tail_tm[0:3, :]).then_inc(out_sem, 16)
            pool.dma_start(conv_s[0].rearrange("b w c -> (b w) c"), tail_tm[3:27, :]).then_inc(out_sem, 16)
            pool.wait_ge(st_ready, 2)
            pool.dma_start(gdn_p[0, 0].rearrange("h d e -> d h e"), Sp[:, :, :]).then_inc(out_sem, 16)
            freed(pool, f"ss{HEADS - 1}1")
            pool.dma_start(gdn_s[0].rearrange("b h d e -> d (b h) e"), Sg[:, :, :]).then_inc(out_sem, 16)
            pool.wait_ge(out_sem, 64)
            pool.dma_start(x_tm[:, 0:2, :], x_prompt[0].rearrange("(s p) d -> p s d", p=128)).then_inc(s_x2, 16)
            pool.dma_start(x_tm[0:64, 2, :], x_sample.rearrange("b t d -> (b t) d")).then_inc(s_x2, 16)
            pool.dma_start(Sg[0:EXPERTS, 0:8, :], b_down[0].rearrange("e (a b) -> e a b", b=128)).then_inc(s_late, 16)
            pool.dma_start(Sg[:, 8:12, :], b_gate_up[0].rearrange("e (m j) -> (e m) j", j=128)
                           .rearrange("(g p) j -> p g j", p=128)).then_inc(s_late, 16)
            pool.dma_start(gla_p[0, 0].rearrange("h d e -> (h d) e").rearrange("(n p) e -> p n e", p=128),
                           Slp[:, :, :]).then_inc(out_sem, 16)
            freed(pool, f"gss{HEADS - 1}1")
            pool.dma_start(gla_s[0].rearrange("b h d e -> (b h d) e").rearrange("(n p) e -> p n e", p=128),
                           Sl[:, :, :]).then_inc(out_sem, 16)
            full(pool, f"ub{KD - 1}")
            pool.dma_start(oAb[:, 0:D], norm2_w.to_broadcast([128, D])).then_inc(s_late, 16)
            pool.dma_start(oBb[:, 0:D], norm_f_w.rearrange("(a d) -> a d", a=1).to_broadcast([128, D])).then_inc(s_late, 16)
            full(pool, "lg2")
            step(pool.memset(y_sl, 0.0))
            step(pool.memset(GTs, 0.0), gtr_done)

        @block.tensor
        def _(pe):
            seen = []

            def take(name):
                assert psum_order()[len(seen)] == name, (name, psum_order()[len(seen)])
                seen.append(name)
                b, u = PSUM_USE[name]
                if u:
                    pe.wait_ge(pfree[b], u)
                return bank[b]

            def done(ins, name):
                ins.then_inc(pfull[PSUM_USE[name][0]], 1)

            def panel(i, k):
                return slot(i % MIX).rearrange("p (k n) -> p k n", k=k)

            def panel_in(i):
                pe.wait_ge(wfull[i % MIX], 16 * (i // MIX + 1))

            def fm(name, i, c0, rhs, kk=KD, m=128):
                o = take(name)
                w = panel(i, kk)
                for k in range(kk):
                    mm = pe.matmul(o[0:m, 0:TOK], w[:, k, c0:c0 + m], rhs[:, k, :], start=(k == 0), stop=(k == kk - 1))
                return mm

            pe.wait_ge(consts, 2)
            pe.wait_ge(s_rows, 16 * 6)
            o = take("cols")
            done(pe.transpose(o[:, 0:60], rows[0:60, :], ident[0:60, 0:60]), "cols")
            o = take("cst")
            for t in range(QT):
                mm = pe.transpose(o[:, 24 * t:24 * t + 24], cst_rows[:, 128 * t:128 * t + 128], ident[0:24, 0:24])
            done(mm, "cst")
            for s in range(3):
                n = TILE_N[s]
                pe.wait_ge(xs_ready, s + 1)
                for f in range(2):
                    o = take(f"xT{s}{f}")
                    for k in range(4):
                        mm = pe.transpose(o[:, 128 * k:128 * k + n], x_tm[0:n, s, 512 * f + 128 * k:512 * f + 128 * k + 128],
                                          ident[0:n, 0:n])
                    done(mm, f"xT{s}{f}")
            freed(pe, "xT21")
            for t in range(QT):
                panel_in(t // 2)
                done(fm(f"qkv{t}", t // 2, 128 * (t % 2), hT), f"qkv{t}")
            pe.wait_ge(s_small, 48)
            o = take("ab")
            for s in range(3):
                n = TILE_N[s]
                for k in range(KD):
                    mm = pe.matmul(o[0:n, 24 * s:24 * s + 24], hT[:, k, TILE_0[s]:TILE_0[s] + n], w_small[:, k, :],
                                   start=(k == 0), stop=(k == KD - 1))
            done(mm, "ab")
            def norm_qk(t):
                pe.wait_ge(sq_ready, t + 1)
                o = take(f"nrm{t}")
                src = (oA if t < 4 else oB)[:, t % 4, :]
                done(pe.matmul(o[:, 0:TOK], ones[:, :], src, start=True, stop=True), f"nrm{t}")

            def z(t):
                panel_in(P_Z + t // 2)
                done(fm(f"z{t}", P_Z + t // 2, 128 * (t % 2), hT), f"z{t}")

            def halves(o, lhs, w, start, stop, width=512):
                for f in range(2):
                    mm = pe.matmul(o[64 * f:64 * f + 64, 0:width], lhs, w[f] if isinstance(w, list) else
                                   w[:, width * f:width * f + width], start=start, stop=stop)
                return mm

            def vb(s):
                n = TILE_N[s]
                panel_in(P_VB)
                panel_in(P_VB + 1)
                o = take(f"vb{s}")
                for k in range(KD if s == 2 else 0):
                    mm = halves(o, hT[:, k, PROMPT:TOK], [panel(P_VB + f, KD)[:, k, :] for f in range(2)], k == 0,
                                k == KD - 1, 256)
                for f in range(2 if s < 2 else 0):
                    for k in range(KD):
                        mm = pe.matmul(o[0:n, 256 * f:256 * f + 256], hT[:, k, TILE_0[s]:TILE_0[s] + n],
                                       panel(P_VB + f, KD)[:, k, :], start=(k == 0), stop=(k == KD - 1))
                done(mm, f"vb{s}")

            for t in range(4):
                norm_qk(t)
            pe.wait_ge(lr_ready, 1)
            o = take("lr")
            for s in range(3):
                n = TILE_N[s]
                mm = pe.transpose(o[0:RANK, TILE_0[s]:TILE_0[s] + n], lr_tm[0:n, s, :], ident[0:n, 0:n])
            done(mm, "lr")
            panel_in(P_QB)
            for t in range(2):
                done(fm(f"qb{t}", P_QB, 128 * t, hT), f"qb{t}")
            freed(pe, "lr")
            for t in range(2):
                o = take(f"gk{t}")
                done(pe.matmul(o[:, 0:TOK], gk_up[:, 128 * t:128 * t + 128], lrT[:, :], start=True, stop=True), f"gk{t}")
            for t in range(4, 8):
                norm_qk(t)
            panel_in(P_KB)
            for t in range(2):
                done(fm(f"kb{t}", P_KB, 128 * t, hT), f"kb{t}")
            for t in range(3):
                z(t)

            def gla_level(lv):
                pe.wait_ge(lev_ready, lv + 1)
                for s in range(3 if lv == 0 else 2):
                    n, a = TILE_N[s], TILE_0[s]
                    for r in range(2):
                        o = p3(take(f"L{lv}{s}{r}"), 2, 128)
                        for hp in range(2):
                            mm = pe.matmul(o[0:n, hp, 0:n], kt[64 * r:64 * r + 64, lv % 2, hp, a:a + n],
                                           qt[64 * r:64 * r + 64, lv % 2, hp, a:a + n], start=True, stop=True)
                        done(mm, f"L{lv}{s}{r}")

            gla_level(0)
            pe.wait_ge(consts, 3)
            pe.wait_ge(g_ready, 1)
            o = take("gc")
            for s in range(3):
                n = TILE_N[s]
                tri = triu if s < 2 else tri8
                mm = pe.matmul(o[0:n, 8 * s:8 * s + 4], tri[0:n, 0:n], g_tm[0:n, s, :], start=True, stop=True)
                lhs = ones[0:n, 0:n] if s < 2 else b8[0:n, 0:n]
                mm = pe.matmul(o[0:n, 8 * s + 4:8 * s + 8], lhs, g_tm[0:n, s, :], start=True, stop=True)
            done(mm, "gc")
            z(3)
            gla_level(1)
            vb(0)
            pe.wait_ge(tails_ready, 1)
            for g in range(3):
                o = take(f"tail{g}")
                for t in range(4):
                    mm = pe.transpose(o[0:27, 128 * t:128 * t + 128], tails[:, 4 * g + t, :], ident[:, :])
                done(mm, f"tail{g}")
            gla_level(2)
            vb(1)
            gla_level(3)
            vb(2)
            pe.wait_ge(kd_ready, 1)
            for s in range(3):
                n, a = TILE_N[s], TILE_0[s]
                o = p3(take(f"gT{s}"), 2, 128)
                for hp in range(2):
                    mm = pe.transpose(o[0:n, hp, :], ek[:, hp, a:a + n], ident[:, :])
                done(mm, f"gT{s}")

            def gla_out(s):
                n, a = TILE_N[s], TILE_0[s]
                pe.wait_ge(at_ready, min(s + 1, 2))
                freed(pe, f"vb{s}")
                if s == 1:
                    pe.wait_ge(qg_ready, 1)
                    freed(pe, "gs0")
                for r in range(2):
                    o = p3(take(f"ob{s}{r}"), 2, 128)
                    for hp in range(2):
                        h = 2 * hp + r
                        mm = pe.matmul(o[:, hp, 0:n], vTM[:, s, 128 * h:128 * h + 128], ATg[:, s, h, 0:n],
                                       start=True, stop=(s != 1), skip_group_check=(s == 2))
                        if s == 1:
                            mm = pe.matmul(o[:, hp, 0:n], Slp[64 * r:64 * r + 64, hp, :],
                                           eq[64 * r:64 * r + 64, hp, a:a + n], start=False, stop=True)
                        if s == 2:
                            for b in range(BATCHES):
                                mm = pe.matmul(o[:, hp, 8 * b:8 * b + 8], Sl[64 * r:64 * r + 64, 2 * b + hp, :],
                                               eq[64 * r:64 * r + 64, hp, a + 8 * b:a + 8 * b + 8], start=False,
                                               stop=True, skip_group_check=True)
                    done(mm, f"ob{s}{r}")
                if s < 2:
                    freed(pe, f"gT{s}")
                    o = p3(take(f"gs{s}"), 2, 256)
                    for hp in range(2):
                        mm = pe.matmul(o[:, hp, :], kdG[s][0:n, 128 * hp:128 * hp + 128],
                                       vTM[0:n, s, 256 * hp:256 * hp + 256], start=True, stop=True)
                    done(mm, f"gs{s}")

            pe.wait_ge(s_state, 32)
            for h in range(HEADS):
                for nm, col in (("gB", g_tm), ("bB", beta)):
                    o = take(f"{nm}{h}")
                    for s in range(3):
                        n = TILE_N[s]
                        rhs = ident if nm == "bB" else (triu if s < 2 else tri8)
                        mm = pe.matmul(o[:, TILE_0[s]:TILE_0[s] + n], col[0:n, s, h:h + 1].to_broadcast([n, 128]),
                                       rhs[0:n, 0:n], start=True, stop=True)
                    done(mm, f"{nm}{h}")
                panel_in(P_GB + h // 2)
                done(fm(f"g{h}", P_GB + h // 2, 128 * (h % 2), hT), f"g{h}")
                if h < 3:
                    gla_out(h)
            pe.wait_ge(qk_ready, 8)
            for s in range(3):
                n = TILE_N[s]
                o = p3(take(f"kT{s}"), HEADS, 128)
                for h in range(HEADS):
                    mm = pe.transpose(o[0:n, h, :], qkv[:, 4 + h, TILE_0[s]:TILE_0[s] + n], ident[:, :])
                done(mm, f"kT{s}")
            for h in range(HEADS):
                pe.wait_ge(osq_ready, h + 1)
                o = take(f"om{h}")
                done(pe.matmul(o[:, 0:TOK], ones[:, :], gsq[:, h, :], start=True, stop=True), f"om{h}")
            pe.wait_ge(kb_ready, HEADS)
            for s in range(3):
                n, a = TILE_N[s], TILE_0[s]
                for nm in "AQ":
                    o = p3(take(f"{nm}{s}"), HEADS, 128)
                    for h in range(HEADS):
                        rhs = oA[:, h, a:a + n] if nm == "A" else qkv[:, h, a:a + n]
                        mm = pe.matmul(o[0:n, h, 0:n], qkv[:, 4 + h, a:a + n], rhs, start=True, stop=True)
                    done(mm, f"{nm}{s}")
            for s in range(3):
                n = TILE_N[s]
                pe.wait_ge(t2t_ready, s + 1)
                o = p3(take(f"t2{s}"), HEADS, 128)
                for h in range(HEADS):
                    mm = pe.transpose(o[0:n, h, 0:n], TT[0:n, s, h, 0:n], ident[0:n, 0:n])
                done(mm, f"t2{s}")
            lts = 0
            for b in LEVELS[1:]:
                tiles = [s for s in range(3) if b in levels_of(s)]
                for s in tiles:
                    n = TILE_N[s]
                    lts += 1
                    pe.wait_ge(lt_ready, lts)
                    if b == 2:
                        freed(pe, f"t2{s}")
                    else:
                        freed(pe, f"Z{s}{b // 2}")
                    o = p3(take(f"X{s}{b}"), HEADS, 128)
                    for h in range(HEADS):
                        mm = pe.matmul(o[0:n, h, 0:n], LT[0:n, s, h, 0:n], T_[0:n, s, h, 0:n], start=True, stop=True)
                    done(mm, f"X{s}{b}")
                for s in tiles:
                    n = TILE_N[s]
                    freed(pe, f"X{s}{b}")
                    if b != levels_of(s)[-1]:
                        o = p3(take(f"Y{s}{b}"), HEADS, 128)
                        for h in range(HEADS):
                            mm = pe.matmul(o[0:n, h, 0:n], TT[0:n, s, h, 0:n], X1[0:n, s, h, 0:n], start=True, stop=True)
                        done(mm, f"Y{s}{b}")
                    o = p3(take(f"Z{s}{b}"), HEADS, 128)
                    for h in range(HEADS):
                        mm = pe.matmul(o[0:n, h, 0:n], X1[0:n, s, h, 0:n], TT[0:n, s, h, 0:n], start=True, stop=True)
                    done(mm, f"Z{s}{b}")

            def gate(nm, m):
                f, i = m // 4, (m % 4) // 2
                q = P_M + 2 * i if f == 0 else P_M + 6 + 4 * i
                if nm == "gb":
                    q += 1
                panel_in(q)
                done(fm(f"{nm}{m}", q, 128 * (m % 2), hT), f"{nm}{m}")

            def rhs_rows(s, src, off):
                n = TILE_N[s]
                o = p3(take(f"rt{s}"), HEADS, 128)
                for h in range(HEADS):
                    mm = pe.transpose(o[0:n, h, :], src[:, h, off:off + n], ident[:, :])
                done(mm, f"rt{s}")

            def new_values(s):
                n = TILE_N[s]
                freed(pe, f"rt{s}")
                freed(pe, f"Z{s}{levels_of(s)[-1]}")
                o = p3(take(f"v{s}"), HEADS, 128)
                for h in range(HEADS):
                    mm = pe.matmul(o[0:n, h, :], TT[0:n, s, h, 0:n], R[0:n, s, h, :], start=True, stop=True)
                done(mm, f"v{s}")

            def gdn_out(s):
                n = TILE_N[s]
                freed(pe, f"v{s}")
                o = p3(take(f"o{s}"), HEADS, 128)
                for h in range(HEADS):
                    mm = pe.matmul(o[:, h, 0:n], R[0:n, s, h, :], attnT[0:n, s, h, 0:n], start=True, stop=(s != 1))
                    if s == 1:
                        mm = pe.matmul(o[:, h, 0:n], Sp[:, h, :], kbqg[:, 1, h, 128:256], start=False, stop=True)
                done(mm, f"o{s}")

            def new_state(s):
                n = TILE_N[s]
                o = p3(take(f"s{s}"), HEADS, 128)
                for h in range(HEADS):
                    mm = pe.matmul(o[:, h, :], kdT[0:n, s, h, :], R[0:n, s, h, :], start=True, stop=True)
                done(mm, f"s{s}")

            rhs_rows(0, qkv[:, 8:12, :], 0)
            gate("ga", 0)
            new_values(0)
            gate("gb", 0)
            gdn_out(0)
            new_state(0)
            gate("ga", 1)
            freed(pe, "s0")
            o = p3(take("ks1"), HEADS, 128)
            for h in range(HEADS):
                mm = pe.matmul(o[:, h, :], Sp[:, h, :], kbqg[:, 0, h, 128:256], start=True, stop=True)
            done(mm, "ks1")
            gate("gb", 1)
            freed(pe, "ks1")
            rhs_rows(1, LT[:, 1, :, :], 0)
            gate("ga", 2)
            new_values(1)
            gate("gb", 2)
            gdn_out(1)
            new_state(1)
            o = take("ks2")[:, :].rearrange("p (h z t) -> p h z t", h=HEADS, z=2)
            for h in range(HEADS):
                for b in range(BATCHES):
                    mm = pe.matmul(o[:, h, :, 8 * b:8 * b + 8], Sg[:, HEADS * b + h, :],
                                   kbqg[:, :, h, PROMPT + 8 * b:PROMPT + 8 * b + 8], start=True, stop=True)
            done(mm, "ks2")
            freed(pe, "ks2")
            rhs_rows(2, LT[:, 2, :, :], 0)
            new_values(2)
            gdn_out(2)
            gate("ga", 3)
            for h in range(HEADS):
                pe.wait_ge(osq_ready, HEADS + h + 1)
                o = take(f"on{h}")
                done(pe.matmul(o[:, 0:TOK], ones[:, :], osq[:, h, :], start=True, stop=True), f"on{h}")
            gate("gb", 3)

            for m in range(KD):
                if m < HEADS:
                    pe.wait_ge(vm_ready, 2 * m + 1)
                    for f in range(2):
                        o = take(f"ss{m}{f}")
                        done(pe.matmul(o[:, :], kdT[0:64, 2, m, :], VM[0][0:64, 4 * f:4 * f + 4, :], start=True,
                                       stop=True), f"ss{m}{f}")
                    pe.wait_ge(vm_ready, 2 * m + 2)
                    r = 64 * (m % 2)
                    c = 128 * (m // 2) + r
                    for f in range(2):
                        o = take(f"gss{m}{f}")
                        done(pe.matmul(o[r:r + 64, :], kdG[2][0:64, c:c + 64], VM[1][0:64, 4 * f:4 * f + 4, :],
                                       start=True, stop=True), f"gss{m}{f}")
                else:
                    gate("ga", m)
                    gate("gb", m)
                if m == 0:
                    pe.wait_ge(o_ready, 2)
                p = P_M + 4 if m < 4 else P_M + 8
                for nm, q, src in (("ua", p, oA), ("ub", p + 1, oB)):
                    panel_in(q)
                    done(fm(f"{nm}{m}", q, 128 * (m % 4), src, HEADS), f"{nm}{m}")
            pe.wait_ge(mrg_ready, KD)
            for i in range(WO):
                pe.wait_ge(wfull[MIX + i], 16)

            def wo(s, f):
                n, a = TILE_N[s], TILE_0[s]
                o = take(f"wo{s}{f}")
                for k in range(KD):
                    c = D * (k % 2) + 512 * f
                    mm = pe.matmul(o[0:n, :], merged[:, k, a:a + n], slot(MIX + k // 2)[:, c:c + 512],
                                   start=(k == 0), stop=(k == KD - 1))
                done(mm, f"wo{s}{f}")

            def turn_h2(s):
                n = TILE_N[s]
                pe.wait_ge(h2_ready, s + 1)
                for f in range(2):
                    o = p3(take(f"hT{s}{f}"), 4, 128)
                    for k in range(4):
                        mm = pe.transpose(o[:, k, 0:n], h2[0:n, s, 512 * f + 128 * k:512 * f + 128 * k + 128],
                                          ident[0:n, 0:n])
                    done(mm, f"hT{s}{f}")

            def logits(s):
                n, a = TILE_N[s], TILE_0[s]
                freed(pe, f"hT{s}1")
                freed(pe, f"hT{s}0")
                o = take(f"lg{s}")
                for k in range(KD):
                    mm = pe.matmul(o[0:n, 0:EXPERTS], hT[:, k, a:a + n], wr[:, k, :], start=(k == 0), stop=(k == KD - 1))
                done(mm, f"lg{s}")

            wo(0, 0)
            wo(0, 1)
            pe.wait_ge(s_late, 64)
            o = take("bgu")
            for g in range(4):
                mm = pe.transpose(o[:, 128 * g:128 * g + 128], Sg[:, 8 + g, :], ident[:, :])
            done(mm, "bgu")
            wo(1, 0)
            turn_h2(0)
            wo(1, 1)
            pe.wait_ge(s_misc, 64)
            logits(0)
            o = take("wo2")
            for k in range(KD):
                mm = halves(o, merged[:, k, PROMPT:TOK], slot(MIX + k // 2)[:, D * (k % 2):D * (k % 2) + D], k == 0,
                            k == KD - 1)
            done(mm, "wo2")
            turn_h2(1)
            logits(1)
            turn_h2(2)
            logits(2)
            pe.wait_ge(mask_ready, 3)
            for s in range(3):
                n = TILE_N[s]
                o = take(f"sl{s}")
                for q in range(s):
                    pe.matmul(o[0:n, 0:EXPERTS], ones[0:TILE_N[q], 0:n], msk[0:TILE_N[q], q, :], start=(q == 0), stop=False)
                done(pe.matmul(o[0:n, 0:EXPERTS], triu[0:n, 0:n], msk[0:n, s, :], start=(s == 0), stop=True), f"sl{s}")
            o = take("cnt")
            for s in range(3):
                mm = pe.matmul(o[:, 0:EXPERTS], ones[0:TILE_N[s], :], msk[0:TILE_N[s], s, :], start=(s == 0), stop=(s == 2))
            done(mm, "cnt")
            def gather(fs=(0, 1)):
                for f in fs:
                    o = p3(bank[7 - f], 4, 2 * SLOTS)
                    for k in range(4):
                        c = 512 * f + 128 * k
                        for s in range(3):
                            mm = pe.matmul(o[:, k, :], h2[0:TILE_N[s], s, c:c + 128], Psel[0:TILE_N[s], s, :],
                                           start=(s == 0), stop=(s == 2))
                    mm.then_inc(m_full[7 - f], 1)

            def turn_gates():
                for s in range(3):
                    n, a = TILE_N[s], TILE_0[s]
                    mm = pe.transpose(bank[7][:, a:a + n], Gsel[0:n, s, :], ident[0:n, 0:n])
                mm.then_inc(m_full[7], 1)

            def scatter(j0, acc0):
                for j in range(j0, j0 + 3):
                    s, f = j // 2, j % 2
                    n, a = TILE_N[s], TILE_0[s]
                    if j >= 2:
                        pe.wait_ge(acc_done, acc0 + j - 1)
                    pe.matmul(bank[7 - j % 2][0:n, :], GTs[:, a:a + n], y_sl[:, 512 * f:512 * f + 512], start=True,
                              stop=True).then_inc(m_full[7 - j % 2], 1)

            def gate_up(x, e):
                for c in range(KD):
                    pe.wait_ge(wfull[c], e * 16 + 16 * (1 + RING_USES[c]))
                    for q in range(2):
                        mm = halves(bank[PRE[q]], xTe[:, c, SLOTS * x:SLOTS * x + SLOTS],
                                    slot(c)[:, FF * q:FF * q + FF], c == 0, c == KD - 1)
                    mm.then_inc(wfree[c], 1)

            def turn_pre():
                for q in range(2):
                    for j in range(4):
                        mm = pe.transpose(bank[FMB[q]][:, 128 * j:128 * j + 128], pre[:, q, 128 * j:128 * j + 128],
                                          ident[:, :])
                mm.then_inc(t_full, 1)

            def down(x, e):
                for c in range(KD, RING):
                    pe.wait_ge(wfull[c], e * 16 + 16 * (1 + RING_USES[c]))
                    for i in range(2):
                        k = 2 * (c - KD) + i
                        mm = halves(bank[DN[x]], hm[x][:, k % 4, k // 4, :], slot(c)[:, D * i:D * i + D], k == 0,
                                    k == FT - 1)
                    mm.then_inc(wfree[c], 1)

            for b in (6, 7):
                pe.wait_ge(pfree[b], max(u for bb, u in PSUM_USE.values() if bb == b) + 1)
            pe.wait_ge(p_ready, 1)
            gather()
            pe.wait_ge(cnt_ready, 1)
            its = pe.value_load(nit[0:1, 0:1], min_val=PAIRS, max_val=PAIRS * ROUNDS)
            pe.wait_ge(gate_ready, 3)
            o = take("wT")
            for s in range(3):
                n, a = TILE_N[s], TILE_0[s]
                mm = pe.transpose(o[0:EXPERTS, a:a + n], gate_all[0:n, s, 0:EXPERTS], ident[0:n, 0:n])
            done(mm, "wT")
            assert len(seen) == len(psum_order())
            for b in range(6):
                pe.wait_ge(pfree[b], max(u for bb, u in PSUM_USE.values() if bb == b) + 1)
            with pe.Fori(0, its) as n:
                pe.wait_ge(xg_done, n * 2 + 2)
                gate_up(0, n * 2)
                pe.wait_ge(yt_done, n * 2 + 1)
                pe.wait_ge(gtr_done, n + 1)
                scatter(0, n * 6)
                pe.wait_ge(pre_done, n * 2 + 1)
                turn_pre()
                scatter(3, n * 6)
                pe.wait_ge(hm_ready, n * 2 + 1)
                down(0, n * 2)
                gate_up(1, n * 2 + 1)
                pe.wait_ge(p_ready, n + 2)
                pe.wait_ge(acc_done, n * 6 + 5)
                gather((0,))
                pe.wait_ge(pre_done, n * 2 + 2)
                turn_pre()
                pe.wait_ge(acc_done, n * 6 + 6)
                gather((1,))
                pe.wait_ge(xg_done, n * 2 + 3)
                pe.wait_ge(gm_ready, n + 1)
                turn_gates()
                pe.wait_ge(hm_ready, n * 2 + 2)
                down(1, n * 2 + 1)
            pe.wait_ge(xg_done, its * 2 + 2)
            pe.wait_ge(yt_done, its * 2 + 1)
            pe.wait_ge(gtr_done, its + 1)
            scatter(0, its * 6)
            scatter(3, its * 6)

        def b6(n, i):
            return n * 4 + (2 + i)

        def b7(n, i):
            return n * 5 + (2 + i)

        def rms_act(step, src, n, acc, signal, scratch):
            step(nc.scalar.activation(scratch, src, ACT.Square, accum_out=ss[0:n, acc:acc + 1]))
            step(nc.scalar.activation(rs[0:n, acc:acc + 1], ss[0:n, acc:acc + 1], ACT.Sqrt, scale=1.0 / D,
                                      bias=eps[0:n, :]), signal)

        @block.scalar
        def _(act):
            step, free = chain(act, act_c)
            A = nc.scalar.activation

            def inv_roots(names, dst, width, signal):
                for i, name in enumerate(names):
                    o = full(act, name)
                    free(A(dst[:, i, :], o[:, 0:TOK], ACT.Ln, scale=1.0 / width, bias=eps[:, :]), name)
                for i in range(len(names)):
                    step(A(dst[:, i, :], dst[:, i, :], ACT.Exp, scale=-0.5), signal)

            act.wait_ge(consts, 1)
            step(A(rs[:, 7:8], eps[:, :], ACT.Sqrt))
            for s in range(3):
                n = TILE_N[s]
                act.wait_ge(s_x[s], 16)
                rms_act(step, x_tm[0:n, s, :], n, s, rs_ready, h2b[0:n, 0:D])
            def silu_conv(t):
                act.wait_ge(conv_done, t + 1)
                step(A(qkv[:, t, 0:PROMPT], cv[:, t % 2, 0:PROMPT], ACT.Silu))
                v = cv[:, t % 2, CATS:CATN].rearrange("p (b w) -> p b w", w=3 + STEPS)[:, :, 0:STEPS]
                step(A(qkv[:, t, PROMPT:TOK].rearrange("p (b w) -> p b w", w=STEPS), v, ACT.Silu), silu_done)
                if t < 8:
                    step(A((oA if t < 4 else oB)[:, t % 4, :], qkv[:, t, :], ACT.Square), sq_ready)

            for t in range(QT):
                o = full(act, f"qkv{t}")
                step(nc.scalar.copy(cat[:, t, 3:CATS], o[:, 0:PROMPT]))
                v = cat[:, t, CATS:CATN].rearrange("p (b w) -> p b w", w=3 + STEPS)[:, :, 3:]
                free(nc.scalar.copy(v, o[:, PROMPT:TOK].rearrange("p (b w) -> p b w", w=STEPS)), f"qkv{t}")
                if t >= 2:
                    silu_conv(t - 2)
            silu_conv(QT - 2)
            silu_conv(QT - 1)
            o = p3(full(act, "ab"), 3, 24)
            step(nc.scalar.copy(lr_tm[:, 0:2, :], o[:, 0:2, 8:24]))
            step(nc.scalar.copy(lr_tm[0:64, 2, :], o[0:64, 2, 8:24]), lr_ready)
            inv_roots([f"nrm{t}" for t in range(4)], oA, 1.0, nrm_ready)
            o = full(act, "lr")
            free(nc.scalar.copy(lrT[:, :], o[0:RANK, 0:TOK]), "lr")
            for t in range(2):
                o = full(act, f"qb{t}")
                free(nc.scalar.mul(qb3[:, t, :], o[:, 0:TOK], DK_B ** -0.5), f"qb{t}")
            freed(act, "cols")
            for t in range(2):
                o = full(act, f"gk{t}")
                free(A(G3[:, t, :], o[:, 0:TOK], ACT.Identity, bias=cols[:, 58 + t:59 + t]), f"gk{t}")
            step(A(ek[:, :, :], G3[:, :, :], ACT.Abs))
            step(A(ek[:, :, :], ek[:, :, :], ACT.Exp, scale=-1.0))
            step(A(ek[:, :, :], ek[:, :, :], ACT.Ln, bias=ones[:, 0:1]), la_act)
            act.wait_ge(ab_mid, 1)
            step(A(soft[:, :, :], absu[:, :, :], ACT.Exp, scale=-1.0))
            step(A(soft[:, :, :], soft[:, :, :], ACT.Ln, bias=ones[:, 0:1]))
            step(A(beta[:, :, :], ab[:, :, 4:8], ACT.Exp, scale=-1.0))
            act.wait_ge(s_misc, 64)
            step(A(hb[:, 4:8], hb[:, 4:8], ACT.Exp), ab_exp)
            inv_roots([f"nrm{t}" for t in range(4, 8)], oB, 1.0, nrm_ready)
            for t in range(2):
                o = full(act, f"kb{t}")
                free(nc.scalar.copy(kb3[:, t, :], o[:, 0:TOK]), f"kb{t}")

            def level_exp(lv):
                w = TOK if lv in (0, 4) else PROMPT
                act.wait_ge(lev_sub, lv + 1)
                step(A(eq[:, :, 0:w], (G3 if lv == 4 else eq)[:, :, 0:w], ACT.Exp))
                step(A(ek[:, :, 0:w], ek[:, :, 0:w], ACT.Exp), lev_exp)

            def silu_z(t):
                o = full(act, f"z{t}")
                free(A(zg[:, t, :], o[:, 0:TOK], ACT.Silu), f"z{t}")

            def take_vb(s):
                n = TILE_N[s]
                o = full(act, f"vb{s}")
                if s < 2:
                    free(nc.scalar.copy(vTM[0:n, s, :], o[0:n, :]), f"vb{s}")
                else:
                    step(nc.scalar.copy(vTM[0:64, s, 0:256], o[0:64, 0:256]))
                    free(nc.scalar.copy(vTM[0:64, s, 256:512], o[64:128, 0:256]), f"vb{s}")

            level_exp(0)
            for t in range(3):
                silu_z(t)
            level_exp(1)
            freed(act, "gc")
            step(A(kdf[:, :, :], kdf[:, :, :], ACT.Exp))
            step(A(glp[:, :, :], glp[:, :, :], ACT.Exp), kdf_ready)
            silu_z(3)
            level_exp(2)
            take_vb(0)
            for g in range(3):
                o = full(act, f"tail{g}")
                free(nc.scalar.copy(tail_tm[0:27, 512 * g:512 * g + 512], o[0:27, :]), f"tail{g}")
            level_exp(3)
            take_vb(1)
            level_exp(4)
            take_vb(2)
            for s in range(3):
                n = TILE_N[s]
                o = full(act, f"gT{s}")
                free(nc.scalar.copy(kdG[s][0:n, :], o[0:n, 0:256]), f"gT{s}")

            oB_r = oB.rearrange("p (a r) t -> p r a t", r=2)
            for h in range(HEADS):
                o = full(act, f"gB{h}")
                for s in range(3):
                    n, a = TILE_N[s], TILE_0[s]
                    step(A(attnT[0:n, s, h, 0:n], o[0:n, a:a + n], ACT.Exp, bias=gneg[0:n, s, h:h + 1]))
                free(A(kbqg[:, 0, h, :], o[:, 0:TOK], ACT.Exp), f"gB{h}")
                o = full(act, f"g{h}")
                free(A(zg[:, 4 + h, :], o[:, 0:TOK], ACT.Silu), f"g{h}")
                if h == 0:
                    act.wait_ge(qk_ready, 8)
                if h < 3:
                    n, a = TILE_N[h], TILE_0[h]
                    for r in range(2):
                        o = p3(full(act, f"ob{h}{r}"), 2, 128)
                        free(nc.scalar.copy(oB_r[:, r, :, a:a + n], o[:, :, 0:n]), f"ob{h}{r}")
                if h == 0:
                    o = p3(full(act, "gs0"), 2, 256)
                    step(nc.scalar.copy(Slp[0:64, :, :], o[0:64, :, 0:128]))
                    free(nc.scalar.copy(Slp[64:128, :, :], o[64:128, :, 128:256]), "gs0")
            for h in range(HEADS):
                step(A(gsq[:, h, :], oB[:, h, :], ACT.Square), osq_ready)
            inv_roots([f"om{h}" for h in range(HEADS)], gsq, DV, onr_ready)

            def evac(name, dst, n, w=128):
                o = p3(full(act, name), HEADS, 128)
                free(nc.scalar.copy(dst, o[0:n, :, 0:w]), name)

            for s in range(3):
                n = TILE_N[s]
                evac(f"t2{s}", T_[0:n, s, :, 0:n], n, n)
            for b in LEVELS[1:]:
                for s in range(3):
                    if b in levels_of(s):
                        n = TILE_N[s]
                        evac(f"X{s}{b}", X1[0:n, s, :, 0:n], n, n)
            def sigmoid_gate(nm, m):
                o = full(act, f"{nm}{m}")
                free(A((gate_a if nm == "ga" else gate_b)[m % 4], o[:, 0:TOK], ACT.Sigmoid), f"{nm}{m}")

            fills = [[("ga", 0), ("gb", 0)], [("ga", 2), ("gb", 2)], None]
            act.wait_ge(gn_ready, HEADS)
            for s in range(3):
                n, a = TILE_N[s], TILE_0[s]
                evac(f"rt{s}", R[0:n, s, :, :], n)
                if fills[s]:
                    sigmoid_gate(*fills[s][0])
                evac(f"v{s}", R[0:n, s, :, :], n)
                if fills[s]:
                    sigmoid_gate(*fills[s][1])
                if s < 2:
                    evac(f"o{s}", oA[:, :, a:a + n], 128, n)
                if s == 0:
                    evac("s0", Sp[:, :, :], 128)
                    sigmoid_gate("ga", 1)
                    sigmoid_gate("gb", 1)
            freed(act, "o2")
            for h in range(HEADS):
                step(A(osq[:, h, :], oA[:, h, :], ACT.Square), osq_ready)
            sigmoid_gate("ga", 3)
            inv_roots([f"on{h}" for h in range(HEADS)], osq, DV, onr_ready)
            sigmoid_gate("gb", 3)
            for m in range(4, KD):
                act.wait_ge(mrg_ready, m - 3)
                sigmoid_gate("ga", m)
                sigmoid_gate("gb", m)

            def norm2(s):
                n = TILE_N[s]
                if s < 2:
                    freed(act, f"wo{s}0")
                    freed(act, f"wo{s}1")
                else:
                    freed(act, "wo2")
                rms_act(step, x_tm[0:n, s, :], n, 3 + s, x2_rs, zgb[0:n, 0:D])

            def take_h2(s):
                n, a = TILE_N[s], TILE_0[s]
                for f in range(2):
                    o = p3(full(act, f"hT{s}{f}"), 4, 128)
                    free(nc.scalar.copy(hT[:, 4 * f:4 * f + 4, a:a + n], o[:, :, 0:n]), f"hT{s}{f}")

            def route_weights(s):
                n = TILE_N[s]
                act.wait_ge(route_max, s + 1)
                step(A(gate_all[0:n, s, 0:EXPERTS], lgt[0:n, s, :], ACT.Exp, bias=rneg[0:n, s, 0:1]))
                step(A(rg4[0:n, s, :], rt8[0:n, s, 0:TOP], ACT.Exp, bias=rneg[0:n, s, 0:1],
                       accum_out=rneg[0:n, s, 1:2]), route_exp)

            norm2(0)
            o = full(act, "bgu")
            free(nc.scalar.copy(bcol[:, :], o[:, :]), "bgu")
            take_h2(0)
            norm2(1)
            o = full(act, "wo2")
            step(nc.scalar.copy(wo_half, o[64:128, :]), half_ready)
            take_h2(1)
            norm2(2)
            take_h2(2)
            act.wait_ge(gtr_done, 1)
            step(nc.scalar.copy(y_sl[0:EXPERTS, :], bdn), yt_done)
            for s in range(3):
                route_weights(s)

            def link(ins, s, value):
                ins.then_inc(s, 1)
                act.wait_ge(s, value)

            def take_tokens(f, value, done):
                b = 7 - f
                act.wait_ge(m_full[b], value)
                link(nc.scalar.copy(xTe[:, 4 * f:4 * f + 4, :], p3(bank[b], 4, 128)), xg_done, done)

            def take_pre(x, n):
                act.wait_ge(wfree[KD - 1], n * 2 + (x + 1))
                link(nc.scalar.copy(pre[:, 0, :], bank[PRE[0]][:, :]), m_act, n * 4 + (2 * x + 1))
                link(nc.scalar.copy(pre[:, 1, :], bank[PRE[1]][:, :]), pre_done, n * 2 + (x + 1))

            def sigmoid(x, n):
                act.wait_ge(pre_sig, n * 2 + (x + 1))
                link(A(sbuf_[:, :, :, :], gbuf[:, :, :, :], ACT.Sigmoid, scale=ALPHA), sg_ready, n * 2 + (x + 1))

            def take_y(x, n):
                act.wait_ge(wfree[RING - 1], n * 2 + (x + 1))
                for f in range(2):
                    ins = nc.scalar.copy(y_sl[SLOTS * x:SLOTS * x + SLOTS, 512 * f:512 * f + 512],
                                         bank[DN[x]][64 * f:64 * f + 64, :])
                    if f == 0:
                        link(ins, m_act, n * 4 + (2 * x + 2))
                    else:
                        link(ins, yt_done, n * 2 + (x + 2))

            act.wait_ge(cnt_ready, 1)
            its = act.value_load(nit[0:1, 0:1], min_val=PAIRS, max_val=PAIRS * ROUNDS)
            take_tokens(0, 1, 1)
            take_tokens(1, 1, 2)
            o = full(act, "wT")
            free(nc.scalar.copy(GTs[0:EXPERTS, :], o[0:EXPERTS, 0:TOK]), "wT")
            with act.Fori(0, its) as n:
                take_pre(0, n)
                sigmoid(0, n)
                take_y(0, n)
                take_pre(1, n)
                take_tokens(0, b7(n, 3), n * 2 + 3)
                sigmoid(1, n)
                take_tokens(1, b6(n, 3), n * 2 + 4)
                act.wait_ge(m_full[7], b7(n, 4))
                link(nc.scalar.copy(GTs[:, :], bank[7][:, 0:TOK]), gtr_done, n + 2)
                take_y(1, n)
            step(A(rs[:, 7:8], eps[:, :], ACT.Sqrt))
            for s in range(3):
                n = TILE_N[s]
                act.wait_ge(acc_done, its * 6 + (2 * s + 2))
                rms_act(step, x_tm[0:n, s, :], n, s, fin_act, zgb[0:n, 0:D])

        @block.vector
        def _(dve):
            step, free = chain(dve, dve_c)
            V = nc.vector
            TTo, TS, STT = V.tensor_tensor, V.tensor_scalar, V.scalar_tensor_tensor

            step(V.memset(kdf[:, :, :], 0.0))
            o = full(dve, "cols")
            free(V.tensor_copy(cols[:, 0:60], o[:, 0:60]), "cols")
            step(V.memset(cat[:, :, 0:3], 0.0))
            o = full(dve, "cst")
            v = cat[:, :, CATS:CATN].rearrange("p t (b w) -> p t b w", w=3 + STEPS)[:, :, :, 0:3]
            free(V.tensor_copy(v, o[:, 0:24 * QT].rearrange("p (t b w) -> p t b w", t=QT, w=3)), "cst")
            for s in range(3):
                n = TILE_N[s]
                dve.wait_ge(rs_ready, s + 1)
                step(V.reciprocal(rs[0:n, s:s + 1], rs[0:n, s:s + 1]))
                step(TS(x_tm[0:n, s, :], x_tm[0:n, s, :], rs[0:n, s:s + 1], None, ALU.mult), xs_ready)
            for s in range(3):
                n, a = TILE_N[s], TILE_0[s]
                for f in range(2):
                    o = p3(full(dve, f"xT{s}{f}"), 4, 128)
                    free(TTo(hT[:, 4 * f:4 * f + 4, a:a + n], o[:, :, 0:n], last(cols[:, 4 * f:4 * f + 4], n), ALU.mult),
                         f"xT{s}{f}")
            for t in range(QT):
                freed(dve, f"qkv{t}")
                if t >= 2:
                    dve.wait_ge(silu_done, t - 1)
                c = cv[:, t % 2, 0:CONVN]
                step(TS(c, cat[:, t, 0:CONVN], cols[:, 8 + t:9 + t], None, ALU.mult))
                for j in range(1, 4):
                    step(STT(out=c, in0=cat[:, t, j:j + CONVN], scalar=cols[:, 8 + QT * j + t:9 + QT * j + t], in1=c,
                             op0=ALU.mult, op1=ALU.add), conv_done if j == 3 else None)
            step(V.tensor_copy(tails[:, :, 0:3], cat[:, :, PROMPT:PROMPT + 3]))
            v = cat[:, :, CATS:CATN].rearrange("p t (b w) -> p t b w", w=3 + STEPS)[:, :, :, STEPS:]
            step(V.tensor_copy(tails[:, :, 3:27].rearrange("p t (b w) -> p t b w", w=3), v), tails_ready)

            dve.wait_ge(consts, 3)
            o = full(dve, "ab")
            dve.wait_ge(lr_ready, 1)
            step(V.tensor_copy(ab[:, 0:2, :], p3(o, 3, 24)[:, 0:2, 0:8]))
            free(V.tensor_copy(ab[0:64, 2, :], o[0:64, 48:56]), "ab")
            dve.wait_ge(s_misc, 64)
            step(TTo(u_dt[:, :, :], ab[:, :, 0:4], mid(hb[:, 0:4], 3), ALU.add))
            step(STT(out=absu[:, :, :], in0=u_dt[:, :, :], scalar=-1.0, in1=u_dt[:, :, :], op0=ALU.mult, op1=ALU.max),
                 ab_mid)

            def normalise(t):
                dve.wait_ge(nrm_ready, t + 1)
                r = (oA if t < 4 else oB)[:, t % 4, :]
                step(STT(out=qkv[:, t, :], in0=qkv[:, t, :], scalar=DK_A ** -0.5 if t < 4 else 1.0, in1=r, op0=ALU.mult,
                         op1=ALU.mult), qk_ready)

            for t in range(4):
                normalise(t)
            step(V.memset(vTM[64:128, 2, :], 0.0))
            step(V.memset(ATg[64:128, 2, :, :], 0.0))
            dve.wait_ge(la_act, 1)
            step(STT(out=eq[:, :, :], in0=G3[:, :, :], scalar=0.0, in1=ek[:, :, :], op0=ALU.min, op1=ALU.subtract))
            for t in range(2):
                step(V.tensor_tensor_scan(G3[:, t, :], rst[:, :], eq[:, t, :], 0.0, ALU.mult, ALU.add))
            step(TS(G3[:, :, :], G3[:, :, :], 1.0 / GATE_NORM, None, ALU.mult))

            def blocks(t, a, w, b):
                return t[:, :, a:a + w].rearrange("p f (n b) -> p f n b", b=b)

            def differences(parts, signal):
                for i, (a, w, b, r) in enumerate(parts):
                    g = blocks(G3, a, w, b)
                    ref = g[:, :, :, r:r + 1].to_broadcast([128, 2, w // b, b])
                    if signal:
                        step(TTo(blocks(eq, a, w, b), g, ref, ALU.subtract))
                    step(TTo(blocks(ek, a, w, b), ref, g, ALU.subtract), lev_sub if i == len(parts) - 1 else None)

            def level_differences(lv):
                b = 8 << lv
                differences([(0, PROMPT, 16, 0), (PROMPT, TOK - PROMPT, 8, 0)] if lv == 0 else
                            [(0, PROMPT, 2 * b, b - 1)], True)

            def level_operands(lv):
                w = TOK if lv == 0 else PROMPT
                dve.wait_ge(lev_exp, lv + 1)
                if lv >= 2:
                    full(dve, f"L{lv - 2}{1 if lv > 2 else 2}1")
                step(STT(out=qt[:, lv % 2, :, 0:w], in0=eq[:, :, 0:w], scalar=1.0, in1=qb3[:, :, 0:w], op0=ALU.min,
                         op1=ALU.mult))
                if lv == 0:
                    step(TTo(kt[:, 0, :, :], ek[:, :, :], kb3[:, :, :], ALU.mult), lev_ready)
                else:
                    step(STT(out=kt[:, lv % 2, :, 0:w], in0=ek[:, :, 0:w], scalar=1.0, in1=kb3[:, :, 0:w], op0=ALU.min,
                             op1=ALU.mult), lev_ready)

            def attention(lv):
                for s in range(3 if lv == 0 else 2):
                    n = TILE_N[s]
                    m = (tri16 if s < 2 else tri8) if lv == 0 else lvm[lv + 3]
                    for r in range(2):
                        o = p3(full(dve, f"L{lv}{s}{r}"), 2, 128)
                        dst = ATg[0:n, s, :, :].rearrange("p (a r) c -> p r a c", r=2)[:, r, :, 0:n]
                        if lv == 0:
                            free(TTo(dst, o[0:n, :, 0:n], mid(m[0:n, 0:n], 2), ALU.mult), f"L{lv}{s}{r}")
                        else:
                            free(TTo(Lp[0:n, :, 0:n], o[0:n, :, 0:n], mid(m[0:n, 0:n], 2), ALU.mult), f"L{lv}{s}{r}")
                            step(TTo(dst, dst, Lp[0:n, :, 0:n], ALU.add), at_ready if lv == 3 and r == 1 else None)

            level_differences(0)
            dve.wait_ge(ab_exp, 1)
            step(STT(out=soft[:, :, :], in0=u_dt[:, :, :], scalar=0.0, in1=soft[:, :, :], op0=ALU.max, op1=ALU.add))
            step(STT(out=g_tm[:, :, :], in0=soft[:, :, :], scalar=-1.0, in1=mid(hb[:, 4:8], 3), op0=ALU.mult,
                     op1=ALU.mult))
            step(TS(beta[:, :, :], beta[:, :, :], 1.0, None, ALU.add))
            step(V.reciprocal(beta[:, :, :], beta[:, :, :]), g_ready)
            freed(dve, "kb0")
            freed(dve, "kb1")
            level_operands(0)
            level_differences(1)
            attention(0)
            level_operands(1)
            level_differences(2)
            o = full(dve, "gc")
            for s in range(3):
                n = TILE_N[s]
                step(TS(gneg[0:n, s, :], o[0:n, 8 * s:8 * s + 4], -1.0, None, ALU.mult))
                step(TTo(kdf[0:n, s, :], o[0:n, 8 * s + 4:8 * s + 8], gneg[0:n, s, :], ALU.add))
            free(V.tensor_copy(glp[:, :, :], o[:, 0:16].rearrange("p (s z h) -> p s z h", s=2, z=2)[:, :, 1, :]), "gc")
            attention(1)
            level_operands(2)
            level_differences(3)
            attention(2)
            level_operands(3)
            differences([(0, PROMPT, 128, 127), (PROMPT, TOK - PROMPT, 8, 7)], False)
            attention(3)
            dve.wait_ge(lev_exp, 5)
            step(V.tensor_copy(gll[:, :, 0:2], blocks(eq, 0, PROMPT, 128)[:, :, :, 127]))
            step(V.tensor_copy(gll[:, :, 2:10], blocks(eq, PROMPT, TOK - PROMPT, 8)[:, :, :, 7]))
            step(TTo(ek[:, :, :], ek[:, :, :], kb3[:, :, :], ALU.mult), kd_ready)
            step(TTo(eq[:, :, :], eq[:, :, :], qb3[:, :, :], ALU.mult), qg_ready)
            for t in range(4, 8):
                normalise(t)
            for h in range(HEADS):
                freed(dve, f"gB{h}")
                step(V.tensor_copy(glb[:, h, :], kbqg[:, 0, h, PROMPT:TOK].rearrange("p (b w) -> p b w", w=8)[:, :, 7]))
                step(TTo(kbqg[:, 1, h, :], kbqg[:, 0, h, :], qkv[:, h, :], ALU.mult))
                o = full(dve, f"bB{h}")
                step(TTo(qkv[:, 8 + h, :], o[:, 0:TOK], qkv[:, 8 + h, :], ALU.mult))
                free(TTo(oA[:, h, :], o[:, 0:TOK], qkv[:, 4 + h, :], ALU.mult), f"bB{h}")
                step(TTo(kbqg[:, 0, h, :], kbqg[:, 0, h, :], oA[:, h, :], ALU.mult), kb_ready)
                if h == 2:
                    o = p3(full(dve, "gs1"), 2, 256)
                    step(TTo(Slp[:, :, :], Slp[:, :, :], last(gll[:, :, 1], 128), ALU.mult))
                    step(TTo(Slp[0:64, :, :], Slp[0:64, :, :], o[0:64, :, 0:128], ALU.add))
                    free(TTo(Slp[64:128, :, :], Slp[64:128, :, :], o[64:128, :, 128:256], ALU.add), "gs1")
            for s in range(3):
                n = TILE_N[s]
                m = triu if s < 2 else tri8
                step(STT(out=attnT[0:n, s, :, 0:n], in0=attnT[0:n, s, :, 0:n], scalar=1.0, in1=mid(m[0:n, 0:n], HEADS),
                         op0=ALU.min, op1=ALU.mult))
            dve.wait_ge(kdf_ready, 1)
            dve.wait_ge(out_sem, 32)
            for s in range(3):
                n = TILE_N[s]
                o = p3(full(dve, f"kT{s}"), HEADS, 128)
                free(TTo(kdT[0:n, s, :, :], o[0:n, :, :], last(kdf[0:n, s, :], 128), ALU.mult), f"kT{s}")
            for s in range(3):
                n = TILE_N[s]
                o = p3(full(dve, f"A{s}"), HEADS, 128)
                free(TTo(AT[0:n, s, :, 0:n], o[0:n, :, 0:n], attnT[0:n, s, :, 0:n], ALU.mult), f"A{s}")
                o = p3(full(dve, f"Q{s}"), HEADS, 128)
                free(TTo(attnT[0:n, s, :, 0:n], o[0:n, :, 0:n], attnT[0:n, s, :, 0:n], ALU.mult), f"Q{s}")

            def level(s, i, signal=None):
                n = TILE_N[s]
                step(TTo(LT[0:n, s, :, 0:n], AT[0:n, s, :, 0:n], mid(lvm[i][0:n, 0:n], HEADS), ALU.mult), signal)

            dve.wait_ge(silu_done, QT)
            full(dve, "tail2")
            for s in range(3):
                n = TILE_N[s]
                level(s, 0)
                step(TTo(TT[0:n, s, :, 0:n], mid(ident[0:n, 0:n], HEADS), LT[0:n, s, :, 0:n], ALU.subtract), t2t_ready)
            for s in range(3):
                level(s, 1, lt_ready)
            for i, b in enumerate(LEVELS):
                for s in range(3):
                    if i == 0 or b not in levels_of(s):
                        continue
                    n = TILE_N[s]
                    final = b == levels_of(s)[-1]
                    full(dve, f"X{s}{b}")
                    if not final:
                        level(s, i + 1, lt_ready)
                        o = p3(full(dve, f"Y{s}{b}"), HEADS, 128)
                        free(TTo(T_[0:n, s, :, 0:n], T_[0:n, s, :, 0:n], o[0:n, :, 0:n], ALU.subtract), f"Y{s}{b}")
                    o = p3(full(dve, f"Z{s}{b}"), HEADS, 128)
                    free(TTo(TT[0:n, s, :, 0:n], TT[0:n, s, :, 0:n], o[0:n, :, 0:n], ALU.subtract), f"Z{s}{b}")
                if b in (8, 16, 32, 64):
                    h = (8, 16, 32, 64).index(b)
                    dve.wait_ge(onr_ready, h + 1)
                    step(TTo(oB[:, h, :], oB[:, h, :], gsq[:, h, :], ALU.mult), gn_ready)
            o = p3(full(dve, "ks1"), HEADS, 128)
            free(TTo(LT[:, 1, :, :], qkv[:, 8:12, 128:256], o[:, :, :], ALU.subtract), "ks1")
            o = p3(full(dve, "s1"), HEADS, 128)
            step(TTo(Sp[:, :, :], Sp[:, :, :], last(glp[:, 1, :], 128), ALU.mult))
            free(TTo(Sp[:, :, :], Sp[:, :, :], o[:, :, :], ALU.add), "s1")
            o = full(dve, "ks2")[:, :].rearrange("p (h z t) -> p h z t", h=HEADS, z=2)
            step(V.tensor_copy(oA[:, :, PROMPT:TOK], o[:, :, 1, :]), st_ready)
            free(TTo(LT[:, 2, :, 0:64], qkv[:, 8:12, PROMPT:TOK], o[:, :, 0, :], ALU.subtract), "ks2")
            o = p3(full(dve, "o2"), HEADS, 128)
            free(TTo(oA[:, :, PROMPT:TOK], oA[:, :, PROMPT:TOK], o[:, :, 0:64], ALU.add), "o2")
            Sg4 = Sg[:, :, :].rearrange("p (b h) e -> p b h e", h=HEADS)
            Sl4 = Sl[:, :, :].rearrange("p (b a) e -> p b a e", a=2)

            def spread(h):
                for i, v in enumerate((R[0:64, 2, h, :], vTM[0:64, 2, 128 * h:128 * h + 128])):
                    if h:
                        full(dve, ("ss" if i == 0 else "gss") + f"{h - 1}1")
                    step(TTo(VM[i][0:64, :, :], mid(v, BATCHES), last(bsel[0:64, :], 128), ALU.mult), vm_ready)

            def sample_states(h):
                r, hp = 64 * (h % 2), h // 2
                for f in range(2):
                    st = Sg4[:, 4 * f:4 * f + 4, h, :]
                    step(TTo(st, st, last(glb[:, h, 4 * f:4 * f + 4], 128), ALU.mult),
                         st_ready if h == 0 and f == 0 else None)
                    o = p3(full(dve, f"ss{h}{f}"), 4, 128)
                    free(TTo(st, st, o, ALU.add), f"ss{h}{f}")
                for f in range(2):
                    st = Sl4[r:r + 64, 4 * f:4 * f + 4, hp, :]
                    step(TTo(st, st, last(gll[r:r + 64, hp, 2 + 4 * f:6 + 4 * f], 128), ALU.mult))
                    o = p3(full(dve, f"gss{h}{f}"), 4, 128)
                    free(TTo(st, st, o[r:r + 64, :, :], ALU.add), f"gss{h}{f}")

            for h in range(HEADS):
                step(STT(out=oB[:, h, :], in0=oB[:, h, :], scalar=cols[:, 57:58], in1=zg[:, 4 + h, :], op0=ALU.mult,
                         op1=ALU.mult), o_ready if h == HEADS - 1 else None)
            spread(0)
            for h in range(HEADS):
                dve.wait_ge(onr_ready, HEADS + h + 1)
                step(TTo(oA[:, h, :], oA[:, h, :], osq[:, h, :], ALU.mult))
                step(STT(out=oA[:, h, :], in0=oA[:, h, :], scalar=cols[:, 56:57], in1=zg[:, h, :], op0=ALU.mult,
                         op1=ALU.mult), o_ready if h == HEADS - 1 else None)

            for m in range(KD):
                if m < HEADS:
                    sample_states(m)
                    if m + 1 < HEADS:
                        spread(m + 1)
                freed(dve, f"ga{m}")
                freed(dve, f"gb{m}")
                o = full(dve, f"ua{m}")
                free(TTo(gate_a[m % 4], o[:, 0:TOK], gate_a[m % 4], ALU.mult), f"ua{m}")
                o = full(dve, f"ub{m}")
                free(TTo(gate_b[m % 4], o[:, 0:TOK], gate_b[m % 4], ALU.mult), f"ub{m}")
                step(TTo(merged[:, m, :], gate_a[m % 4], gate_b[m % 4], ALU.add), mrg_ready)
            dve.wait_ge(s_x2, 32)

            def add_rows(name, s, f):
                n = TILE_N[s]
                o = full(dve, name)
                v = x_tm[0:n, s, 512 * f:512 * f + 512]
                free(TTo(v, v, o[0:n, :], ALU.add), name)

            def norm_rows(s):
                n = TILE_N[s]
                dve.wait_ge(x2_rs, s + 1)
                step(V.reciprocal(rs[0:n, 3 + s:4 + s], rs[0:n, 3 + s:4 + s]))
                step(STT(out=h2[0:n, s, :], in0=x_tm[0:n, s, :], scalar=rs[0:n, 3 + s:4 + s], in1=n2b[0:n, :],
                         op0=ALU.mult, op1=ALU.mult), h2_ready)

            def top4(s):
                n = TILE_N[s]
                o = full(dve, f"lg{s}")
                free(TTo(lgt[0:n, s, :], o[0:n, 0:EXPERTS], brt[0:n, :], ALU.add), f"lg{s}")
                step(V.max(rt8[0:n, s, :], lgt[0:n, s, :]))
                step(TS(rneg[0:n, s, 0:1], rt8[0:n, s, 0:1], -1.0, None, ALU.mult), route_max)
                step(V.max_index(ri8[0:n, s, :], rt8[0:n, s, :], lgt[0:n, s, :]))
                step(V.tensor_copy(rif[0:n, s, :], ri8[0:n, s, :]))
                for k in range(TOP):
                    step(STT(out=msk[0:n, s, :], in0=iota[0:n, 0:EXPERTS], scalar=rif[0:n, s, k:k + 1],
                             in1=msk[0:n, s, :], op0=ALU.is_equal, op1=ALU.add), mask_ready if k == TOP - 1 else None)

            def gates(s):
                n = TILE_N[s]
                dve.wait_ge(route_exp, s + 1)
                step(V.reciprocal(rneg[0:n, s, 1:2], rneg[0:n, s, 1:2]))
                gate = gate_all[0:n, s, 0:EXPERTS]
                step(STT(out=gate, in0=gate, scalar=rneg[0:n, s, 1:2], in1=msk[0:n, s, :], op0=ALU.mult,
                         op1=ALU.mult), gate_ready)

            def gates_again(s):
                n = TILE_N[s]
                more = gate_all[0:n, s, EXPERTS:EXPERTS * ROUNDS].rearrange("p (r e) -> p r e", e=EXPERTS)
                step(V.tensor_copy(more, mid(gate_all[0:n, s, 0:EXPERTS], ROUNDS - 1)))

            step(V.memset(msk[:, :, :], 0.0))
            step(V.memset(gate_all[:, :, :], 0.0))
            step(V.memset(slot_all[:, :, :], -1.0))
            add_rows("wo00", 0, 0)
            add_rows("wo01", 0, 1)
            dve.wait_ge(s_late, 64)
            norm_rows(0)
            add_rows("wo10", 1, 0)
            add_rows("wo11", 1, 1)
            norm_rows(1)
            top4(0)
            dve.wait_ge(half_ready, 1)
            step(TTo(x_tm[0:64, 2, 512:D], x_tm[0:64, 2, 512:D], wo_half, ALU.add))
            o = full(dve, "wo2")
            free(TTo(x_tm[0:64, 2, 0:512], x_tm[0:64, 2, 0:512], o[0:64, :], ALU.add), "wo2")
            norm_rows(2)
            top4(1)
            top4(2)
            for s in range(3):
                n = TILE_N[s]
                o = full(dve, f"sl{s}")
                free(TTo(slot1[0:n, s, :], o[0:n, 0:EXPERTS], msk[0:n, s, :], ALU.mult), f"sl{s}")
                step(TS(slot_all[0:n, s, 0:EXPERTS], slot1[0:n, s, :], -1.0, None, ALU.add))

            def link(ins, s, value):
                ins.then_inc(s, 1)
                dve.wait_ge(s, value)

            def one_hot(dst, x, col):
                c = slot_all[:, :, bass.ds(col, 1)].to_broadcast([128, 3, SLOTS])
                return TTo(dst[:, :, SLOTS * x:SLOTS * x + SLOTS], mid(iota[:, :], 3), c, ALU.is_equal)

            step(one_hot(Psel, 0, 0))
            step(one_hot(Psel, 1, 1), p_ready)
            o = full(dve, "cnt")
            free(V.reduce_max(cmax[:, 0:1], o[:, 0:EXPERTS], AX_X), "cnt")
            step(TS(cmax[:, 1:1 + ROUNDS], iota[:, 0:ROUNDS], float(SLOTS), cmax[:, 0:1], ALU.mult, ALU.is_lt))
            step(V.reduce_sum(cmax[:, 6:7], cmax[:, 1:1 + ROUNDS], AX_X))
            step(TS(nit[:, 0:1], cmax[:, 6:7], float(PAIRS), None, ALU.mult))
            step(TS(nit[:, 1:2], cmax[:, 6:7], float(EXPERTS), None, ALU.mult), cnt_ready)
            for s in range(3):
                gates(s)
            for s in range(3):
                gates_again(s)
            for s in range(3):
                n = TILE_N[s]
                for r in range(1, ROUNDS):
                    step(TS(slot_all[0:n, s, EXPERTS * r:EXPERTS * r + EXPERTS], slot1[0:n, s, :], -1.0 - SLOTS * r, None,
                            ALU.add))
            its = dve.value_load(nit[0:1, 0:1], min_val=PAIRS, max_val=PAIRS * ROUNDS)
            CH = 12

            def scattered(n, j0):
                for j in range(j0, j0 + 3):
                    s, f = j // 2, j % 2
                    rows_n = TILE_N[s]
                    if j % 2:
                        dve.wait_ge(m_full[6], b6(n, j // 2))
                    else:
                        dve.wait_ge(m_full[7], b7(n, j // 2))
                    v = x_tm[0:rows_n, s, 512 * f:512 * f + 512]
                    link(TTo(v, v, bank[7 - j % 2][0:rows_n, :], ALU.add), acc_done, n * 6 + (j + 1))

            with dve.Fori(0, its) as n:
                k = [0]

                def inner(ins):
                    k[0] += 1
                    link(ins, m_dve, n * CH + k[0])

                dve.wait_ge(m_full[6], n * 4 + 1)
                inner(one_hot(Psel, 0, n * 2 + 2))
                link(one_hot(Psel, 1, n * 2 + 3), p_ready, n + 2)
                dve.wait_ge(m_full[7], n * 5 + 1)
                for y in range(2):
                    inner(one_hot(Gsel, y, n * 2 + y))
                    g = gate_all[:, :, bass.ds(n * 2 + y, 1)].to_broadcast([128, 3, SLOTS])
                    part = Gsel[:, :, SLOTS * y:SLOTS * y + SLOTS]
                    if y == 0:
                        inner(TTo(part, part, g, ALU.mult))
                    else:
                        link(TTo(part, part, g, ALU.mult), gm_ready, n + 1)
                scattered(n, 0)
                for x in range(2):
                    dve.wait_ge(t_full, n * 2 + (x + 1))
                    e = n % PAIRS
                    for dst, b, c0 in ((gbuf, FMB[0], 0), (ubuf, FMB[1], FT)):
                        bias = bcol[:, bass.ds(e * 32 + (16 * x + c0), FT)].rearrange("p (h j) -> p j h", h=2)
                        bias = bias.unsqueeze(3).to_broadcast([128, 4, 2, SLOTS])
                        src = bank[b][:, :].rearrange("p (j h t) -> p j h t", j=4, h=2)
                        inner(TTo(dst[:, :, :, :], src, bias, ALU.add))
                        if c0 == 0:
                            link(TS(gbuf[:, :, :, :], gbuf[:, :, :, :], LIMIT, None, ALU.min), pre_sig, n * 2 + (x + 1))
                    inner(TS(ubuf[:, :, :, :], ubuf[:, :, :, :], LIMIT, -LIMIT, ALU.min, ALU.max))
                    inner(STT(out=ubuf[:, :, :, :], in0=ubuf[:, :, :, :], scalar=1.0, in1=gbuf[:, :, :, :], op0=ALU.add,
                              op1=ALU.mult))
                    dve.wait_ge(sg_ready, n * 2 + (x + 1))
                    link(TTo(hm[x], ubuf[:, :, :, :], sbuf_[:, :, :, :], ALU.mult), hm_ready, n * 2 + (x + 1))
                    if x == 0:
                        scattered(n, 3)
                assert k[0] == CH, k
            scattered(its, 0)
            scattered(its, 3)
            for s in range(3):
                n = TILE_N[s]
                dve.wait_ge(fin_act, s + 1)
                step(V.reciprocal(rs[0:n, s:s + 1], rs[0:n, s:s + 1]))
                step(STT(out=x_tm[0:n, s, :], in0=x_tm[0:n, s, :], scalar=rs[0:n, s:s + 1], in1=nfb[0:n, :],
                         op0=ALU.mult, op1=ALU.mult), fin_dve)


_INS = ["x_prompt", "x_sample", "state_gdn", "state_gdn_conv", "state_gla", "norm1_w", "w_in", "conv_w", "a_log",
        "dt_bias", "gdn_norm_w", "gla_gk_up", "gla_gk_b", "gla_norm_w", "w_up_a", "w_up_b", "w_o", "norm2_w",
        "w_router", "b_router", "w_gate_up", "b_gate_up", "w_down", "b_down", "norm_f_w"]
_OUTS = [(1, PROMPT, D), (BATCHES, STEPS, D), (1, 1, HEADS, DK_A, DV), (1, 1, 3, QKV), (1, 1, HEADS, DK_B, DV),
         (1, BATCHES, HEADS, DK_A, DV), (1, BATCHES, 3, QKV), (1, BATCHES, HEADS, DK_B, DV)]


def kernel(**inputs):
    import numpy as _np
    import concourse.bacc as _bacc
    from concourse import mybir as _mybir
    from concourse.bass_utils import run_bass_kernel_spmd as _run

    nc = _bacc.Bacc("TRN2", target_bir_lowering=False, num_devices=1)
    arrays, args = {}, []
    for name in _INS:
        a = _np.ascontiguousarray(inputs[name])
        arrays[f"in_{name}_dram"] = a
        args.append(nc.dram_tensor(f"in_{name}_dram", a.shape, _mybir.dt.from_np(a.dtype), kind="ExternalInput").ap())
    for i, shape in enumerate(_OUTS):
        args.append(nc.dram_tensor(f"out_{i}_dram", shape, F32, kind="ExternalOutput").ap())
    build(nc, *args)
    r = _run(nc, [arrays], core_ids=[0])
    return tuple(r.results[0][f"out_{i}_dram"] for i in range(len(_OUTS)))
```
